# Optimizing a Trainium2 kernel written in Bass

```python
import jax
import jax.numpy as jnp
from jax import lax
import numpy as np

D_MODEL = 1024
BATCH = 1
SEQ = 256
DEPTH = 2
DEC_BATCH = 8
DEC_SEQ = 8
PAST_LEN = 256
PAGE_SIZE = 128

N_EVEN = (DEPTH + 1) // 2
N_ODD = DEPTH // 2
MOBA_HEADS = 8
MOBA_HEAD_DIM = 64
MOBA_BLOCK = 256
MOBA_TOPK = 3
QUERY_BLOCK = 128
ROPE_THETA = 10000.0
HG_HEADS = 4
HG_DK = 128
HG_DV = 128
HG_CHUNK = 64
LRU_WIDTH = D_MODEL
LRU_HEADS = 4
LRU_BLOCK = LRU_WIDTH // LRU_HEADS
CONV_WIDTH = 4
LRU_C = 8.0
N_GROUPS = 4
EXPERTS_PER_GROUP = 4
N_EXPERTS = N_GROUPS * EXPERTS_PER_GROUP
EXPERT_TOPK = 2
EXPERT_FF = D_MODEL // 2
NORM_EPS = 1e-6

MOBA_WIDTH = MOBA_HEADS * MOBA_HEAD_DIM
HG_KEY_WIDTH = HG_HEADS * HG_DK
HG_VAL_WIDTH = HG_HEADS * HG_DV
EVEN_SPLITS = (MOBA_WIDTH, 2 * MOBA_WIDTH, 3 * MOBA_WIDTH,
               3 * MOBA_WIDTH + HG_KEY_WIDTH,
               3 * MOBA_WIDTH + 2 * HG_KEY_WIDTH,
               3 * MOBA_WIDTH + 2 * HG_KEY_WIDTH + HG_VAL_WIDTH)
EVEN_IN_WIDTH = 3 * MOBA_WIDTH + 2 * HG_KEY_WIDTH + 2 * HG_VAL_WIDTH
EVEN_OUT_WIDTH = MOBA_WIDTH + HG_VAL_WIDTH

kernel_name = 'hybrid_moba_hgrn2_rglru_hmoe_step'

F32 = jnp.float32

def _rmsnorm(x, w):
    xf = x.astype(F32)
    y = xf * lax.rsqrt(jnp.mean(xf * xf, axis=-1, keepdims=True) + NORM_EPS)
    return (y * w.astype(F32)).astype(x.dtype)

def _largest_divisor(n, cap):
    d = min(n, cap)
    while n % d:
        d -= 1
    return d

def _rope(x, pos):
    half = x.shape[-1] // 2
    inv_freq = jnp.power(ROPE_THETA, -jnp.arange(half, dtype=F32) / half)
    ang = pos.astype(F32)[:, None] * inv_freq[None, :]
    cos = jnp.cos(ang)[None, :, None, :]
    sin = jnp.sin(ang)[None, :, None, :]
    xf = x.astype(F32)
    x1, x2 = xf[..., :half], xf[..., half:]
    return jnp.concatenate([x1 * cos - x2 * sin, x2 * cos + x1 * sin], axis=-1).astype(x.dtype)

def _moba_one_seq(q, k, v, q_pos0):
    n_heads, lq, dh = q.shape
    n_blk = k.shape[1] // MOBA_BLOCK
    kb = k.reshape(n_heads, n_blk, MOBA_BLOCK, dh)
    vb = v.reshape(n_heads, n_blk, MOBA_BLOCK, dh)
    k_mean = jnp.mean(kb.astype(F32), axis=2)
    qb = _largest_divisor(lq, QUERY_BLOCK)
    n_sel = min(MOBA_TOPK, n_blk)
    scale = dh ** -0.5
    blk_ids = jnp.arange(n_blk)
    in_blk = jnp.arange(MOBA_BLOCK)
    head_ids = jnp.arange(n_heads)[:, None, None]

    def one_block(i):
        qf = lax.dynamic_slice_in_dim(q, i * qb, qb, axis=1).astype(F32)
        pos = q_pos0 + i * qb + jnp.arange(qb)
        own = pos // MOBA_BLOCK
        gate = jnp.einsum('hqd,hnd->hqn', qf, k_mean)
        gate = jnp.where(blk_ids[None, None, :] < own[None, :, None], gate, -jnp.inf)
        _, sel = lax.top_k(gate, n_sel)
        sel_ok = sel < own[None, :, None]
        blocks = jnp.concatenate(
            [sel, jnp.broadcast_to(own[None, :, None], (n_heads, qb, 1))], axis=-1)
        blk_ok = jnp.concatenate([sel_ok, jnp.ones((n_heads, qb, 1), dtype=bool)], axis=-1)
        key_pos = blocks[..., None] * MOBA_BLOCK + in_blk
        mask = blk_ok[..., None] & (key_pos <= pos[None, :, None, None])
        k_g = kb[head_ids, blocks].astype(F32)
        v_g = vb[head_ids, blocks].astype(F32)
        s = jnp.einsum('hqd,hqnkd->hqnk', qf, k_g) * scale
        s = jnp.where(mask, s, -jnp.inf).reshape(n_heads, qb, -1)
        p = jax.nn.softmax(s, axis=-1).reshape(n_heads, qb, n_sel + 1, MOBA_BLOCK)
        return jnp.einsum('hqnk,hqnkd->hqd', p, v_g).astype(q.dtype)

    out = lax.map(one_block, jnp.arange(lq // qb))
    return out.transpose(1, 0, 2, 3).reshape(n_heads, lq, dh)

def _moba(q, k, v, q_pos0):
    b_sz, seq_len, n_heads, dh = q.shape
    pad = (-k.shape[1]) % MOBA_BLOCK
    k = jnp.pad(k, ((0, 0), (0, pad), (0, 0), (0, 0)))
    v = jnp.pad(v, ((0, 0), (0, pad), (0, 0), (0, 0)))
    qt, kt, vt = q.transpose(0, 2, 1, 3), k.transpose(0, 2, 1, 3), v.transpose(0, 2, 1, 3)
    out = lax.map(lambda a: _moba_one_seq(a[0], a[1], a[2], q_pos0), (qt, kt, vt))
    return out.transpose(0, 2, 1, 3).reshape(b_sz, seq_len, n_heads * dh)

def _gated_linear_recurrence(q, k, v, log_f, s0):
    b_sz, seq_len, n_heads, _ = q.shape
    dv = v.shape[-1]
    cl = _largest_divisor(seq_len, HG_CHUNK)
    n_chunks = seq_len // cl

    def to_chunks(a):
        return a.reshape(b_sz, n_chunks, cl, n_heads, a.shape[-1]).transpose(1, 0, 3, 2, 4)

    causal = jnp.tril(jnp.ones((cl, cl), dtype=bool))[None, None, :, :, None]

    def step(s, inp):
        qc, kc, vc, lc = inp
        b = jnp.cumsum(lc, axis=2)
        b_last = b[:, :, -1:, :]
        o_inter = jnp.einsum('bhtk,bhkv->bhtv', qc * jnp.exp(b), s)
        decay = jnp.exp(jnp.where(causal, b[:, :, :, None, :] - b[:, :, None, :, :], -jnp.inf))
        scores = jnp.einsum('bhtsk,bhsk->bhts', qc[:, :, :, None, :] * decay, kc)
        o = o_inter + jnp.einsum('bhts,bhsv->bhtv', scores, vc)
        s_new = (jnp.exp(b_last[:, :, 0, :])[..., None] * s
                 + jnp.einsum('bhsk,bhsv->bhkv', kc * jnp.exp(b_last - b), vc))
        return s_new, o

    s_last, o = lax.scan(step, s0, (to_chunks(q), to_chunks(k), to_chunks(v), to_chunks(log_f)))
    o = o.transpose(1, 0, 3, 2, 4).reshape(b_sz, seq_len, n_heads, dv)
    return o, s_last

def _hgrn2(q, f_pre, i, g, lb, norm_w, s0):
    b_sz, seq_len, _ = q.shape
    qf = jax.nn.silu(q.astype(F32)).reshape(b_sz, seq_len, HG_HEADS, HG_DK)
    f = lb + (1.0 - lb) * jax.nn.sigmoid(f_pre.astype(F32)).reshape(b_sz, seq_len, HG_HEADS, HG_DK)
    kf = 1.0 - f
    log_f = jnp.log(f)
    vf = i.astype(F32).reshape(b_sz, seq_len, HG_HEADS, HG_DV)
    o, s_last = _gated_linear_recurrence(qf, kf, vf, log_f, s0.astype(F32))
    o = o * lax.rsqrt(jnp.mean(o * o, axis=-1, keepdims=True) + NORM_EPS) * norm_w.astype(F32)
    o = o * jax.nn.silu(g.astype(F32).reshape(b_sz, seq_len, HG_HEADS, HG_DV))
    return o.reshape(b_sz, seq_len, HG_VAL_WIDTH).astype(q.dtype), s_last

def _even_mixer(u, pos0, past_k, past_v, w_in, w_out, lb, norm_w, s0):
    b_sz, seq_len, _ = u.shape
    q_a, k_a, v_a, q_b, f_b, i_b, g_b = jnp.split(u @ w_in, EVEN_SPLITS, axis=-1)
    pos = pos0 + jnp.arange(seq_len, dtype=jnp.int32)
    q_a = _rope(q_a.reshape(b_sz, seq_len, MOBA_HEADS, MOBA_HEAD_DIM), pos)
    k_a = _rope(k_a.reshape(b_sz, seq_len, MOBA_HEADS, MOBA_HEAD_DIM), pos)
    v_a = v_a.reshape(b_sz, seq_len, MOBA_HEADS, MOBA_HEAD_DIM)
    if past_k is None:
        k_all, v_all = k_a, v_a
    else:
        k_all = jnp.concatenate([past_k.astype(k_a.dtype), k_a], axis=1)
        v_all = jnp.concatenate([past_v.astype(v_a.dtype), v_a], axis=1)
    o_a = _moba(q_a, k_all, v_all, pos0)
    o_b, s_last = _hgrn2(q_b, f_b, i_b, g_b, lb, norm_w, s0)
    out = jnp.concatenate([o_a, o_b], axis=-1) @ w_out
    return out, k_a, v_a, s_last

def _rg_lru(x, wa, ba, wx, bx, lam, h0):
    b_sz, seq_len, width = x.shape
    xf = x.astype(F32)
    xb = xf.reshape(b_sz, seq_len, LRU_HEADS, LRU_BLOCK)
    r = jax.nn.sigmoid(jnp.einsum('blhi,hij->blhj', xb, wa.astype(F32)).reshape(b_sz, seq_len, width) + ba.astype(F32))
    ig = jax.nn.sigmoid(jnp.einsum('blhi,hij->blhj', xb, wx.astype(F32)).reshape(b_sz, seq_len, width) + bx.astype(F32))
    log_a = -LRU_C * r * jax.nn.softplus(-lam.astype(F32))
    a = jnp.exp(log_a)
    gx = jnp.sqrt(-jnp.expm1(2.0 * log_a)) * (ig * xf)

    def step(h, inp):
        a_t, u_t = inp
        h = a_t * h + u_t
        return h, h

    h_last, hs = lax.scan(step, h0.astype(F32), (a.transpose(1, 0, 2), gx.transpose(1, 0, 2)))
    return hs.transpose(1, 0, 2).astype(x.dtype), h_last

def _griffin_block(u, w_in, conv_w, conv_b, wa, ba, wx, bx, lam, w_out, conv0, h0):
    seq_len = u.shape[1]
    proj = u @ w_in
    gate_br = jax.nn.gelu(proj[..., :LRU_WIDTH], approximate=True)
    rec = proj[..., LRU_WIDTH:]
    hist = jnp.concatenate([conv0.astype(rec.dtype), rec], axis=1)
    conv = conv_b
    for tap in range(CONV_WIDTH):
        conv = conv + hist[:, tap:tap + seq_len] * conv_w[tap]
    conv_state = hist[:, seq_len:]
    y, h_last = _rg_lru(conv, wa, ba, wx, bx, lam, h0)
    out = (y * gate_br) @ w_out
    return out, conv_state, h_last

def _hier_moe(u, rg_w, rg_b, re_w, re_b, w1, w3, w2):
    b_sz, seq_len, d = u.shape
    t = u.reshape(b_sz * seq_len, d)
    g_prob = jax.nn.softmax((t @ rg_w + rg_b).astype(F32), axis=-1)
    g_val, g_idx = lax.top_k(g_prob, 1)
    e_logits = (t @ re_w + re_b).astype(F32).reshape(-1, N_GROUPS, EXPERTS_PER_GROUP)
    e_logits = jnp.take_along_axis(e_logits, g_idx[:, :, None], axis=1)[:, 0]
    e_prob = jax.nn.softmax(e_logits, axis=-1)
    e_val, e_idx = lax.top_k(e_prob, EXPERT_TOPK)
    weights = g_val * e_val / jnp.sum(e_val, axis=-1, keepdims=True)
    expert = g_idx * EXPERTS_PER_GROUP + e_idx
    combine = jnp.sum(jax.nn.one_hot(expert, N_EXPERTS, dtype=F32) * weights[..., None], axis=1)
    h1 = jnp.einsum('td,edf->tef', t, w1)
    h3 = jnp.einsum('td,edf->tef', t, w3)
    act = jax.nn.silu(h1) * h3 * combine[:, :, None].astype(t.dtype)
    y = jnp.einsum('tef,efd->td', act, w2)
    return y.reshape(b_sz, seq_len, d)

def _run_group(x, c, past_k, past_v, hg0, conv0, lru0, ada_w, ada_b, norm_mix, norm_ffn, norm_final,
               w_in_even, w_out_even, hg_lower_bounds, hg_norm_w, w_in_odd, conv_w, conv_b,
               lru_wa, lru_ba, lru_wx, lru_bx, lru_lambda, w_out_odd, router_group_w, router_group_b,
               router_expert_w, router_expert_b, moe_w1, moe_w3, moe_w2):
    pos0 = 0 if past_k is None else past_k.shape[2]
    lbs = jnp.cumsum(jax.nn.softmax(hg_lower_bounds.astype(F32), axis=0), axis=0)
    b_sz = x.shape[0]
    h = x
    k_rows, v_rows, hg_states, conv_states, lru_states = [], [], [], [], []
    for l in range(DEPTH):
        j = l // 2
        mods = (c @ ada_w[l] + ada_b[l]).reshape(b_sz, 1, 6, D_MODEL)
        shift1, scale1, gate1 = mods[:, :, 0], mods[:, :, 1], mods[:, :, 2]
        shift2, scale2, gate2 = mods[:, :, 3], mods[:, :, 4], mods[:, :, 5]
        u = _rmsnorm(h, norm_mix[l]) * (1.0 + scale1) + shift1
        if l % 2 == 0:
            out, k_new, v_new, s_new = _even_mixer(
                u, pos0,
                None if past_k is None else past_k[j],
                None if past_v is None else past_v[j],
                w_in_even[j], w_out_even[j], lbs[j].reshape(HG_HEADS, HG_DK), hg_norm_w[j], hg0[j])
            k_rows.append(k_new)
            v_rows.append(v_new)
            hg_states.append(s_new.astype(x.dtype))
        else:
            out, c_state, h_last = _griffin_block(
                u, w_in_odd[j], conv_w[j], conv_b[j], lru_wa[j], lru_ba[j], lru_wx[j], lru_bx[j],
                lru_lambda[j], w_out_odd[j], conv0[j], lru0[j])
            conv_states.append(c_state)
            lru_states.append(h_last.astype(x.dtype))
        h = h + gate1 * out
        u = _rmsnorm(h, norm_ffn[l]) * (1.0 + scale2) + shift2
        h = h + gate2 * _hier_moe(u, router_group_w[l], router_group_b[l], router_expert_w[l],
                                  router_expert_b[l], moe_w1[l], moe_w3[l], moe_w2[l])
    y = _rmsnorm(h, norm_final)
    return (y, jnp.stack(k_rows), jnp.stack(v_rows), jnp.stack(hg_states),
            jnp.stack(conv_states), jnp.stack(lru_states))

def setup_inputs(seed: int = 0) -> dict:
    key = jax.random.key(seed)
    ks = jax.random.split(key, 36)
    n_pages = PAST_LEN // PAGE_SIZE
    n_used = DEC_BATCH * n_pages
    n_phys = n_used + n_used // 4

    def nrm(k, shape, scale):
        return jax.random.normal(k, shape, F32) * scale

    a_c = jax.random.uniform(ks[26], (N_ODD, LRU_WIDTH), F32, 0.9, 0.999)
    sig = a_c ** (1.0 / LRU_C)
    return {
        'x_prompt': nrm(ks[0], (BATCH, SEQ, D_MODEL), 1.0),
        'x_sample': nrm(ks[1], (DEC_BATCH, DEC_SEQ, D_MODEL), 1.0),
        'c_prompt': nrm(ks[2], (BATCH, D_MODEL), 1.0),
        'c_sample': nrm(ks[3], (DEC_BATCH, D_MODEL), 1.0),
        'cache_k': nrm(ks[4], (N_EVEN, n_phys, PAGE_SIZE, MOBA_HEADS, MOBA_HEAD_DIM), 1.0),
        'cache_v': nrm(ks[5], (N_EVEN, n_phys, PAGE_SIZE, MOBA_HEADS, MOBA_HEAD_DIM), 1.0),
        'state_hgrn': nrm(ks[6], (N_EVEN, DEC_BATCH, HG_HEADS, HG_DK, HG_DV), 0.5),
        'state_conv': nrm(ks[7], (N_ODD, DEC_BATCH, CONV_WIDTH - 1, LRU_WIDTH), 1.0),
        'state_lru': nrm(ks[8], (N_ODD, DEC_BATCH, LRU_WIDTH), 0.5),
        'page_table': jax.random.permutation(ks[9], n_phys)[:n_used].reshape(DEC_BATCH, n_pages).astype(jnp.int32),
        'ada_w': nrm(ks[10], (DEPTH, D_MODEL, 6 * D_MODEL), 0.2 * D_MODEL ** -0.5),
        'ada_b': nrm(ks[11], (DEPTH, 6 * D_MODEL), 0.02),
        'norm_mix': 1.0 + nrm(ks[12], (DEPTH, D_MODEL), 0.02),
        'norm_ffn': 1.0 + nrm(ks[13], (DEPTH, D_MODEL), 0.02),
        'norm_final': 1.0 + nrm(ks[14], (D_MODEL,), 0.02),
        'w_in_even': nrm(ks[15], (N_EVEN, D_MODEL, EVEN_IN_WIDTH), D_MODEL ** -0.5),
        'w_out_even': nrm(ks[16], (N_EVEN, EVEN_OUT_WIDTH, D_MODEL), EVEN_OUT_WIDTH ** -0.5),
        'hg_lower_bounds': nrm(ks[17], (N_EVEN + 1, HG_KEY_WIDTH), 1.0),
        'hg_norm_w': 1.0 + nrm(ks[18], (N_EVEN, HG_DV), 0.02),
        'w_in_odd': nrm(ks[19], (N_ODD, D_MODEL, 2 * LRU_WIDTH), D_MODEL ** -0.5),
        'conv_w': nrm(ks[20], (N_ODD, CONV_WIDTH, LRU_WIDTH), CONV_WIDTH ** -0.5),
        'conv_b': nrm(ks[21], (N_ODD, LRU_WIDTH), 0.02),
        'lru_wa': nrm(ks[22], (N_ODD, LRU_HEADS, LRU_BLOCK, LRU_BLOCK), LRU_BLOCK ** -0.5),
        'lru_ba': nrm(ks[23], (N_ODD, LRU_WIDTH), 0.02),
        'lru_wx': nrm(ks[24], (N_ODD, LRU_HEADS, LRU_BLOCK, LRU_BLOCK), LRU_BLOCK ** -0.5),
        'lru_bx': nrm(ks[25], (N_ODD, LRU_WIDTH), 0.02),
        'lru_lambda': jnp.log(sig) - jnp.log1p(-sig),
        'w_out_odd': nrm(ks[27], (N_ODD, LRU_WIDTH, D_MODEL), LRU_WIDTH ** -0.5),
        'router_group_w': nrm(ks[28], (DEPTH, D_MODEL, N_GROUPS), D_MODEL ** -0.5),
        'router_group_b': nrm(ks[29], (DEPTH, N_GROUPS), 0.01),
        'router_expert_w': nrm(ks[30], (DEPTH, D_MODEL, N_EXPERTS), D_MODEL ** -0.5),
        'router_expert_b': nrm(ks[31], (DEPTH, N_EXPERTS), 0.01),
        'moe_w1': nrm(ks[32], (DEPTH, N_EXPERTS, D_MODEL, EXPERT_FF), D_MODEL ** -0.5),
        'moe_w3': nrm(ks[33], (DEPTH, N_EXPERTS, D_MODEL, EXPERT_FF), D_MODEL ** -0.5),
        'moe_w2': nrm(ks[34], (DEPTH, N_EXPERTS, EXPERT_FF, D_MODEL), EXPERT_FF ** -0.5),
    }

def reference(x_prompt, x_sample, c_prompt, c_sample, cache_k, cache_v, state_hgrn, state_conv, state_lru,
              page_table, ada_w, ada_b, norm_mix, norm_ffn, norm_final, w_in_even, w_out_even,
              hg_lower_bounds, hg_norm_w, w_in_odd, conv_w, conv_b, lru_wa, lru_ba, lru_wx, lru_bx,
              lru_lambda, w_out_odd, router_group_w, router_group_b, router_expert_w, router_expert_b,
              moe_w1, moe_w3, moe_w2):
    dec_b, n_pages = page_table.shape
    past_len = n_pages * cache_k.shape[2]
    past_k = cache_k[:, page_table].reshape(N_EVEN, dec_b, past_len, MOBA_HEADS, MOBA_HEAD_DIM)
    past_v = cache_v[:, page_table].reshape(N_EVEN, dec_b, past_len, MOBA_HEADS, MOBA_HEAD_DIM)
    b_sz = x_prompt.shape[0]
    hg0 = jnp.zeros((N_EVEN, b_sz, HG_HEADS, HG_DK, HG_DV), x_prompt.dtype)
    conv0 = jnp.zeros((N_ODD, b_sz, CONV_WIDTH - 1, LRU_WIDTH), x_prompt.dtype)
    lru0 = jnp.zeros((N_ODD, b_sz, LRU_WIDTH), x_prompt.dtype)
    y_prompt, k_prompt, v_prompt, hgrn_prompt, conv_prompt, lru_prompt = _run_group(
        x_prompt, c_prompt, None, None, hg0, conv0, lru0, ada_w, ada_b, norm_mix, norm_ffn, norm_final,
        w_in_even, w_out_even, hg_lower_bounds, hg_norm_w, w_in_odd, conv_w, conv_b, lru_wa, lru_ba,
        lru_wx, lru_bx, lru_lambda, w_out_odd, router_group_w, router_group_b, router_expert_w,
        router_expert_b, moe_w1, moe_w3, moe_w2)
    y_sample, k_sample, v_sample, hgrn_sample, conv_sample, lru_sample = _run_group(
        x_sample, c_sample, past_k, past_v, state_hgrn, state_conv, state_lru, ada_w, ada_b, norm_mix,
        norm_ffn, norm_final, w_in_even, w_out_even, hg_lower_bounds, hg_norm_w, w_in_odd, conv_w, conv_b,
        lru_wa, lru_ba, lru_wx, lru_bx, lru_lambda, w_out_odd, router_group_w, router_group_b,
        router_expert_w, router_expert_b, moe_w1, moe_w3, moe_w2)
    return (y_prompt, y_sample, k_prompt, v_prompt, k_sample, v_sample, hgrn_prompt, hgrn_sample,
            conv_prompt, conv_sample, lru_prompt, lru_sample)


_drawn_inputs = setup_inputs


def setup_inputs(seed=0):
    import zlib

    import numpy as np

    out = dict(_drawn_inputs(seed))
    spreads = {}
    factors = {'cache_k': 4.293,
     'cache_v': 3.579,
     'norm_mix': 2.909,
     'norm_ffn': 4.068,
     'norm_final': 2.868,
     'hg_norm_w': 8.0,
     'lru_ba': 8.0,
     'lru_bx': 7.409,
     'router_group_b': 8.0,
     'router_expert_b': 8.0}
    for name, (base, spread) in spreads.items():
        noise = np.random.default_rng([zlib.crc32(name.encode()), seed]).standard_normal(out[name].shape)
        drawn = base * np.exp(spread * noise) if base else spread * noise
        out[name] = jnp.asarray(drawn.astype(out[name].dtype))
    for name, factor in factors.items():
        out[name] = (out[name] * factor).astype(out[name].dtype)
    return out
```

```python
from contextlib import ExitStack

import numpy as np

import concourse.bass as bass
from concourse import mybir

P = 128
D = 1024
DT = D // P
NP_TOK, NS_SEQ, S_LEN = 256, 8, 8
NS_TOK = NS_SEQ * S_LEN
T = NP_TOK + NS_TOK
NSEQ = 1 + NS_SEQ
TT = 3
TROWS = (128, 128, 64)
HEADS, DH = 8, 64
PAIRS = HEADS // 2
HG = 4
CH = 8
NCHUNK = T // CH
PAGE = 128
PAST_PAGES = 2
GROUPS, EPG = 4, 4
NE = GROUPS * EPG
FF = 512
FT = FF // P
CONV = 4
N_PHYS = 20
EPS = 1e-6
SCALE = DH ** -0.5
FAR = -1e30

PIECE = 4096
RING = 4
ADA_PIECES = 12
AT_ADA = 0
AT_EVEN = 2 * ADA_PIECES
AT_EVEN_OUT = AT_EVEN + 7
AT_MOE = (AT_EVEN_OUT + 2, AT_EVEN_OUT + 2 + 3 * NE + 7)
AT_ODD = AT_MOE[0] + 3 * NE
AT_LRU = AT_ODD + 4
AT_ODD_OUT = AT_LRU + 1
N_PIECES = AT_MOE[1] + 3 * NE
assert AT_ODD_OUT + 2 == AT_MOE[1] and N_PIECES % RING == 0

C_ADAB = 0
C_NMIX = C_ADAB + 96
C_NFFN = C_NMIX + 16
C_NFIN = C_NFFN + 16
C_LB = C_NFIN + 8
C_HGW = C_LB + 8
C_CONVW = C_HGW + 1
C_CONVB = C_CONVW + 32
C_BA = C_CONVB + 8
C_BX = C_BA + 8
C_LAM = C_BX + 8
N_COLS = C_LAM + 8

K_ID = 0
K_COS = K_ID + P
K_SIN = K_COS + TT * DH
K_MP = K_SIN + TT * DH
K_MS = K_MP + 384
K_CM = K_MS + 256
K_RANK = K_CM + 4
K_EPS = K_RANK + 4
N_CONST = K_EPS + 1

ALU = mybir.AluOpType
ACT = mybir.ActivationFunctionType
F32 = mybir.dt.float32
AX = mybir.AxisListType.X


class Chain:

    def __init__(self, eng, sem):
        self.eng, self.sem, self.n, self.it, self.per = eng, sem, 0, None, 0

    def enter(self, it, per):
        self.it, self.per, self.start = it, per, self.n

    def leave(self, trips):
        assert self.n - self.start == self.per, (self.n - self.start, self.per)
        self.n, self.it = self.start + self.per * trips, None

    def __call__(self, ins):
        ins.then_inc(self.sem, 1)
        self.n += 1
        self.eng.wait_ge(self.sem, self.n if self.it is None else self.it * self.per + self.n)


def build(nc, I, O):
    ctx = ExitStack()
    with ctx:
        sems = {}

        def sem(name):
            if name not in sems:
                sems[name] = ctx.enter_context(nc.semaphore(name))
            return sems[name]

        def sb(name, *shape, dt=F32):
            return ctx.enter_context(nc.sbuf_tensor(name, list(shape), dt))

        ring = [sb(f"ring{s}", P, PIECE) for s in range(RING)]
        w8 = [r[:, :].rearrange("p (k n) -> p k n", k=8) for r in ring]
        w4 = [r[:, :].rearrange("p (k n) -> p k n", k=4) for r in ring]
        hT = sb("hT", P, DT, T)
        uT = sb("uT", P, DT, T)
        tmp = sb("tmp", P, DT, T)
        const = sb("const", P, N_CONST)
        cols = sb("cols", P, N_COLS)
        ones = sb("ones", P, P)
        cT = sb("cT", P, DT, NSEQ)
        mods = sb("mods", P, 2, 48, NSEQ)
        gain = sb("gain", P, 4, DT, NSEQ)
        stat = sb("stat", P, 64)
        diag = sb("diag", P, TT, P)
        rw = sb("rw", P, 2, DT, 20)
        rb = sb("rb", 1, 2, 20)
        pages = sb("pages", 1, 2 * NS_SEQ, dt=mybir.dt.int32)
        SCR = 24800
        scr = sb("scr", P, SCR)
        banks = ctx.enter_context(nc.psum_tensor("banks", [P, 8, 512], F32))
        ps = [banks[:, b, :] for b in range(8)]
        sadd = sb("sadd", P, 2, NS_TOK)

        def carve(at, *shape):
            n = int(np.prod(shape))
            assert at + n <= SCR, (at, n)
            v = scr[:, at:at + n]
            if len(shape) == 1:
                return v
            names = "abcd"[:len(shape)]
            return v.rearrange(f"p ({' '.join(names)}) -> p {' '.join(names)}",
                               **{c: s for c, s in zip(names, shape)})

        ident = const[:, K_ID:K_ID + P]

        B = HG * T
        prj = carve(0, 16, T)
        kf = carve(4 * B, HG, T)
        pre = carve(5 * B, HG, T)
        suf = carve(6 * B, HG, T)
        wlag = [carve((7 + i) * B, HG, T) for i in range(2)]
        xlag = carve(9 * B, HG, T)
        tlag = carve(10 * B, HG, T)
        oB = carve(11 * B, HG, T)
        ktok = carve(7 * B, 2, 512)
        vexp = carve(7 * B + 1024, 2, 4, 512)
        S_END = carve(12 * B, NSEQ, HG, P)
        S_ST = carve(12 * B + NSEQ * 512, 8, HG, P)
        xlag2 = carve(12 * B + NSEQ * 512, HG, T)
        assert 7 * B + 1024 + 4096 <= 11 * B
        odiag = carve(7 * B, TT, HG, P)
        qtok = carve(0, TT, 512)
        ktk = carve(1536, TT, 512)
        vtok = carve(3072, TT, 512)
        qkT = carve(4608, 2, PAIRS, T)
        QX = carve(7168, PAIRS, NS_SEQ, 64)
        KV = carve(9216, 2, 2, 2, 512)
        sc = carve(13312, 2, 384)
        pT = carve(14080, 2, 384)
        sm = carve(14848, 2, 8)
        assert 14912 <= 12 * B
        rt1 = carve(12 * B + NSEQ * 512, 512)
        rt2 = carve(12 * B + NSEQ * 512 + 512, 512)
        mixT = tmp

        flat = banks[:, :, :].rearrange("p b n -> p (b n)")
        gT = carve(0, DT, T)
        recP = carve(2560, DT, NP_TOK + 3)
        recS = carve(4632, DT, NS_SEQ, S_LEN + 3)
        hist = carve(21120, DT, NS_SEQ, 3)
        xc = carve(5336, DT, T)
        rT = carve(7896, DT, T)
        iT = carve(10456, DT, T)
        aT = carve(13016, DT, T)
        t1 = carve(15576, DT, T)
        hs = carve(18136, DT, T)
        lsp = carve(20696, 6, DT)
        lru0 = carve(20760, DT, NS_SEQ)
        ends = carve(20824, DT, NSEQ)
        cst = carve(20900, DT, NSEQ, 3)

        lg = carve(0, TT, 20)
        rt = carve(64, TT, 96)
        comb = carve(400, TT, NE)
        cdiag = carve(448, TT, P)
        cb = carve(832, 2, T)
        sig = carve(1472, 2, T)
        act = carve(2112, 2, FT, T)
        yacc = carve(4672, DT, T)

        def adab(l):
            return cols[:, C_ADAB + 48 * l:C_ADAB + 48 * (l + 1)]

        def shift(s):
            l, w = s // 2, s % 2
            return mods[:, l, 24 * w:24 * w + 8, :]

        def gate(s):
            l, w = s // 2, s % 2
            return mods[:, l, 24 * w + 16:24 * w + 24, :]

        block = ctx.enter_context(nc.Block())

        @block.sync
        def _(sp):
            for s in range(RING):
                sp.dma_start(ring[s][:, :], I["w"][s, :, :]).then_inc(sem(f"piece_in{s}"), 16)
            with sp.Fori(1, N_PIECES // RING) as r:
                for s in range(RING):
                    sp.wait_ge(sem(f"piece_used{s}"), r)
                    sp.dma_start(ring[s][:, :], I["w"][r * RING + s, :, :]).then_inc(sem(f"piece_in{s}"), 16)

        @block.gpsimd
        def _(pool):
            pool.dma_start(pages[:, :], I["pages"]).then_inc(sem("pages_in"), 16)
            pool.memset(ones[:, :], 1.0).then_inc(sem("ones_ready"), 1)
            pool.wait_ge(sem("hgrn_done"), 1)
            pool.dma_start(O["hgrn"], S_END).then_inc(sem("hgrn_stored"), 16)
            pool.wait_ge(sem("pages_in"), 16)
            for b in range(NS_SEQ):
                if b >= 2:
                    pool.wait_ge(sem("spv_used"), b - 1)
                for g in range(PAST_PAGES):
                    pg = pool.value_load(pages[0:1, 2 * b + g:2 * b + g + 1], min_val=0, max_val=N_PHYS - 1)
                    pool.dma_start(KV[:, b % 2, 0, g, :], I["kT"][bass.ds(pg, 1), :, :].rearrange("o p n -> p (o n)"))\
                        .then_inc(sem(f"past_in{b % 2}"), 16)
                    pool.dma_start(KV[:, b % 2, 1, g, :], I["v"][bass.ds(pg, 1), :, :].rearrange("o p n -> p (o n)"))\
                        .then_inc(sem(f"past_in{b % 2}"), 16)
                if b == 1:
                    for n, (name, src) in enumerate((("k", ktk), ("v", vtok))):
                        pool.wait_ge(sem("qkv_ev"), 6 + 3 * n)
                        pool.dma_start(O[name][0:256, :].rearrange("(t p) n -> p t n", p=P), src[:, 0:2, :])\
                            .then_inc(sem("kv_stored"), 16)
                        pool.dma_start(O[name][256:T, :], src[0:64, 2, :]).then_inc(sem("kv_stored"), 16)
            pool.wait_ge(sem("h_ready"), 2)
            pool.dma_start(hist, I["convT"]).then_inc(sem("hist_in"), 16)
            pool.dma_start(lru0, I["lruT"]).then_inc(sem("hist_in"), 16)
            pool.wait_ge(sem("ends_ready"), 1)
            pool.dma_start(O["lruT"], ends).then_inc(sem("ends_stored"), 16)
            pool.dma_start(O["convT"], cst).then_inc(sem("ends_stored"), 16)
            pool.wait_ge(sem("hgrn_stored"), 16)
            pool.wait_ge(sem("kv_stored"), 64)
            pool.wait_ge(sem("ends_stored"), 32)

        @block.scalar
        def _(e):
            for name, dst in (("cT", cT[:, :, :]), ("cols", cols[:, :]), ("const", const[:, :]), ("xT", hT[:, :, :]),
                              ("rw", rw[:, :, :, :]), ("rb", rb[:, :, :])):
                e.dma_start(dst, I[name]).then_inc(sem(f"{name}_in"), 16)
            e.dma_start(S_END[:, 1:NSEQ, :, :], I["s0"]).then_inc(sem("s0_in"), 16)

            def norm(n):
                if n == 0:
                    e.wait_ge(sem("xT_in"), 16)
                    e.wait_ge(sem("const_in"), 16)
                else:
                    e.wait_ge(sem("h_ready"), n)
                for c in range(2):
                    e.activation(tmp[:, 4 * c:4 * c + 4, :], hT[:, 4 * c:4 * c + 4, :], ACT.Square)\
                        .then_inc(sem("sq_ready"), 1)
                e.wait_ge(sem("sumsq_ready"), n + 1)
                e.activation(stat[:, 0:2], ps[7][:, 0:2], ACT.Sqrt, bias=const[:, K_EPS:K_EPS + 1], scale=1.0 / D)\
                    .then_inc(sem("rms_ready"), 1)
                e.activation(stat[0:64, 2:3], ps[7][0:64, 2:3], ACT.Sqrt, bias=const[0:64, K_EPS:K_EPS + 1],
                             scale=1.0 / D).then_inc(sem("rms_ready"), 1)

            def router(l):
                for n, (dst, src) in enumerate(((rt[:, :, 4:8], rt[:, :, 0:4]), (rt[:, :, 41:42], rt[:, :, 40:41]))):
                    e.wait_ge(sem("rexp_in"), 2 * l + n + 1)
                    e.activation(dst, src, ACT.Exp).then_inc(sem("rexp_out"), 1)

            def experts(l):
                def expert(n, it=None):
                    for f in range(FT):
                        k = n * FT + f
                        base = 0 if it is None else it * (4 * FT)
                        e.wait_ge(sem(f"h13_ready{l}"), base + k + 1)
                        if it is not None or k >= 2:
                            e.wait_ge(sem(f"h13_used{l}"), base + k - 1)
                        e.activation(sig[:, f % 2, :], ps[2 * (f % 2)][:, 0:T], ACT.Sigmoid)\
                            .then_inc(sem(f"sig_ready{l}"), 1)
                for n in range(4):
                    expert(n)
                with e.Fori(1, 4) as it:
                    for n in range(4):
                        expert(n, it)

            norm(0)
            e.wait_ge(sem("lb_in"), 1)
            e.activation(stat[:, 8:12], stat[:, 12:16], ACT.Sigmoid).then_inc(sem("lb_ready"), 1)
            for dst, src in ((xlag, 0), (tlag, 1), (wlag[0], 3)):
                e.wait_ge(sem("prj_ev"), 4 * (src + 1))
                e.activation(dst, prj[:, 4 * src:4 * src + 4, :], ACT.Sigmoid).then_inc(sem("hsig_ready"), 1)
            e.wait_ge(sem("inter_ev"), NCHUNK // 4)
            e.activation(tlag, oB, ACT.Square).then_inc(sem("osq_ready"), 1)
            e.wait_ge(sem("osum_ready"), 1)
            e.activation(stat[:, 16:24], ps[7][:, 0:8], ACT.Sqrt, bias=const[:, K_EPS:K_EPS + 1], scale=1.0 / P)\
                .then_inc(sem("orms_ready"), 1)
            e.activation(stat[0:64, 24:28], ps[7][0:64, 8:12], ACT.Sqrt, bias=const[0:64, K_EPS:K_EPS + 1],
                         scale=1.0 / P).then_inc(sem("orms_ready"), 1)
            for h in range(HEADS):
                e.wait_ge(sem("pmax_ready"), h + 1)
                for q, (lo, hi) in enumerate(((0, 128), (128, 384))):
                    e.activation(sc[:, h % 2, lo:hi], sc[:, h % 2, lo:hi], ACT.Exp, bias=sm[:, h % 2, q:q + 1],
                                 accum_out=sm[:, h % 2, 4 + q:5 + q]).then_inc(sem("pexp_ready"), 1)
            for s in range(4):
                e.wait_ge(sem("smax_ready"), s + 1)
                e.activation(sc[:, s % 2, 0:320], sc[:, s % 2, 0:320], ACT.Exp, bias=sm[:, s % 2, 0:1],
                             accum_out=sm[:, s % 2, 4:5]).then_inc(sem("sexp_ready"), 1)
            norm(1)
            router(0)
            experts(0)
            norm(2)
            e.wait_ge(sem("gelu_in"), 1)
            e.activation(t1, t1, ACT.Tanh).then_inc(sem("gelu_out"), 1)
            e.wait_ge(sem("lam_in"), 1)
            e.activation(lsp[:, 1, :], lsp[:, 0, :], ACT.Exp, scale=-1.0).then_inc(sem("lam_out"), 1)
            for m in range(16):
                e.wait_ge(sem("lru_ready"), m + 1)
                dst, b = ((rT, C_BA), (iT, C_BX))[m // 8]
                e.activation(dst[:, m % 8, :], ps[m % 4][:, 0:T], ACT.Sigmoid,
                             bias=cols[:, b + m % 8:b + m % 8 + 1]).then_inc(sem("lru_ev"), 1)
            e.wait_ge(sem("loga_ready"), 1)
            e.activation(aT, rT, ACT.Exp).then_inc(sem("a_ready"), 1)
            e.activation(t1, rT, ACT.Tanh, scale=-1.0).then_inc(sem("a_ready"), 1)
            e.wait_ge(sem("om_ready"), 1)
            e.activation(t1, t1, ACT.Sqrt).then_inc(sem("root_ready"), 1)
            norm(3)
            router(1)
            experts(1)
            norm(4)
            e.wait_ge(sem("y_ready"), 1)
            e.dma_start(O["yT"], uT[:, :, :]).then_inc(sem("y_stored"), 16)
            e.wait_ge(sem("y_stored"), 16)

        @block.tensor
        def _(pe):
            mm = pe.matmul

            def piece(n, rounds=None):
                v = 16 * (n // RING + 1)
                pe.wait_ge(sem(f"piece_in{n % RING}"), v if rounds is None else rounds * 16 + v)

            gone = []

            def used(n):
                gone.append(n % RING)

            def group(out, pairs):
                for i, (a, b) in enumerate(pairs):
                    last = mm(out, a, b, start=(i == 0), stop=(i == len(pairs) - 1))
                    if gone and i < len(pairs) - 1:
                        last.then_inc(sem(f"piece_used{gone.pop(0)}"), 1)
                return last

            def norm(n):
                for c in range(2):
                    pe.wait_ge(sem("sq_ready"), 2 * n + c + 1)
                for t, rows in enumerate(TROWS):
                    last = group(ps[7][0:rows, t:t + 1],
                                 [(tmp[:, k, P * t:P * t + rows], ones[:, 0:1]) for k in range(DT)])
                last.then_inc(sem("sumsq_ready"), 1)
                pe.wait_ge(sem("rdiag_ready"), n + 1)
                for t, rows in enumerate(TROWS):
                    last = mm(ps[6][:, P * t:P * t + rows], ones[0:rows, :], diag[0:rows, t, 0:rows],
                              start=True, stop=True)
                last.then_inc(sem("rstd_ready"), 1)

            def project(at, src, name, n0=0, src_tiles=DT):
                piece(at)
                for m in range(4):
                    n = n0 + m
                    if n >= 4:
                        pe.wait_ge(sem(f"{name}_ev"), n - 3)
                    last = group(ps[n % 4][:, 0:T],
                                 [(w8[at % RING][:, k, P * m:P * m + P], src[:, k, :]) for k in range(DT)])
                    last.then_inc(sem(f"{name}_ps"), 1)
                used(at)

            pe.wait_ge(sem("cT_in"), 16)
            with pe.Fori(0, 2) as l:
                with pe.Fori(0, 3) as r:
                    for j in range(4):
                        piece(j, l * 3 + r)
                        for m in range(4):
                            col = l * 512 + r * 144 + (4 * j + m) * NSEQ
                            last = group(flat[:, bass.ds(col, NSEQ)],
                                         [(w8[j][:, k, P * m:P * m + P], cT[:, k, :]) for k in range(DT)])
                            if m == 3:
                                last.then_inc(sem(f"piece_used{j}"), 1)
            pe.wait_ge(sem("ones_ready"), 1)
            pe.wait_ge(sem("const_in"), 16)
            norm(0)
            pe.wait_ge(sem("u_ready"), 1)
            for i in range(4):
                project(AT_EVEN + i, uT, "prj", 4 * i)
            for d in range(CH):
                X = (xlag, xlag2)[d % 2]
                pe.wait_ge(sem("xlag_ready"), d + 1)
                if d >= 2:
                    pe.wait_ge(sem("lag_ev"), d - 1)
                for h in range(HG):
                    x = X[:, h, :].rearrange("p (c t) -> p c t", t=CH)[:, :, d:CH]
                    o = ps[4 * (d % 2) + h][:, 0:NCHUNK * (CH - d)].rearrange("p (c t) -> p c t", t=CH - d)
                    last = mm(o, ones[:, :], x, start=True, stop=True)
                last.then_inc(sem("lag_ps"), 1)

            def turn(t):
                rows = TROWS[t]
                if t == 0:
                    pe.wait_ge(sem("ktil_ready"), 1)
                for n, src in ((0, suf), (1, prj[:, 8:12, :])):
                    if 2 * t + n >= 1:
                        pe.wait_ge(sem("turn_ev"), 2 * t + n)
                    for h in range(HG):
                        last = pe.transpose(ps[7][0:rows, P * h:P * h + P], src[:, h, P * t:P * t + rows], ident)
                    last.then_inc(sem("turn_ps"), 1)

            def updates(G):
                t, p = G // 4, 32 * (G % 4)
                if G % 4 == 0:
                    pe.wait_ge(sem("turn_ev"), 2 * t + 2)
                for half in range(2):
                    u = 2 * G + half
                    if u >= 3:
                        pe.wait_ge(sem("chain"), u - 2)
                    for h in range(HG):
                        o = ps[2 * (u % 3) + h // 2][:, 256 * (h % 2):256 * (h % 2) + 256]\
                            .rearrange("p (c n) -> p c n", c=2)
                        last = mm(o, ktok[p:p + 32, t % 2, P * h:P * h + P],
                                  vexp[p:p + 32, t % 2, 2 * half:2 * half + 2, P * h:P * h + P],
                                  start=True, stop=True, skip_group_check=True)
                    last.then_inc(sem("upd_ps"), 1)

            def outputs(G):
                if G < 8:
                    pe.wait_ge(sem("chain"), 2 * G + 2)
                if G >= 1:
                    pe.wait_ge(sem("inter_ev"), G)
                for c in range(4):
                    j = 4 * G + c
                    for h in range(HG):
                        S = S_ST[:, j % 8, h, :] if G < 8 else S_END[:, j - 31, h, :]
                        last = mm(ps[6][:, 32 * h + 8 * c:32 * h + 8 * c + 8], S, prj[:, h, 8 * j:8 * j + 8],
                                  start=True, stop=True)
                last.then_inc(sem("inter_ps"), 1)

            pe.wait_ge(sem("lag_ev"), CH)
            turn(0)
            updates(0)
            for G in range(NCHUNK // 4):
                if G % 4 == 1 and G // 4 + 1 < TT:
                    turn(G // 4 + 1)
                if G + 1 < NCHUNK // 4 and G < 8:
                    updates(G + 1)
                if G == 8:
                    outputs(8)
                    updates(9)
                    outputs(9)
                elif G < 8:
                    outputs(G)
            pe.wait_ge(sem("osq_ready"), 1)
            for t, rows in enumerate(TROWS):
                for h in range(HG):
                    last = mm(ps[7][0:rows, 4 * t + h:4 * t + h + 1], tlag[:, h, P * t:P * t + rows], ones[:, 0:1],
                              start=True, stop=True)
            last.then_inc(sem("osum_ready"), 1)
            pe.wait_ge(sem("odiag_ready"), 1)
            for h in range(HG):
                for t, rows in enumerate(TROWS):
                    last = mm(ps[h][:, P * t:P * t + rows], ones[0:rows, :], odiag[0:rows, t, h, 0:rows],
                              start=True, stop=True)
            last.then_inc(sem("orstd_ready"), 1)

            pe.wait_ge(sem("hgrn_done"), 1)
            n = 0
            for i in range(3):
                piece(AT_EVEN + 4 + i)
                for t, rows in enumerate(TROWS):
                    if n >= 6:
                        pe.wait_ge(sem("qkv_ev"), n - 5)
                    last = group(ps[n % 6][0:rows, :], [(uT[:, k, P * t:P * t + rows], w8[(AT_EVEN + 4 + i) % RING][:, k, :])
                                                        for k in range(DT)])
                    last.then_inc(sem("qkv_ps"), 1)
                    n += 1
                used(AT_EVEN + 4 + i)
            for src in (qtok, ktk):
                for t, rows in enumerate(TROWS):
                    pe.wait_ge(sem("qkv_ev"), max(n - 5, 6))
                    for p in range(PAIRS):
                        last = pe.transpose(ps[n % 6][:, P * p:P * p + rows], src[0:rows, t, P * p:P * p + P],
                                            ident[0:rows, 0:rows])
                    last.then_inc(sem("qkv_ps"), 1)
                    n += 1
            qT, kTn = qkT[:, 0, :, :], qkT[:, 1, :, :]
            pe.wait_ge(sem("qkv_ev"), 15)

            def prompt_scores(h):
                p, e = h // 2, 64 * (h % 2)
                if h >= 2:
                    pe.wait_ge(sem("pmask_done"), h - 1)
                o = ps[h % 2]
                mm(o[:, 0:128], qT[e:e + 64, p, 0:128], kTn[e:e + 64, p, 0:128], start=True, stop=True)
                mm(o[:, 128:384], qT[e:e + 64, p, 128:256], kTn[e:e + 64, p, 0:256], start=True, stop=True)\
                    .then_inc(sem("pscore_ps"), 1)

            def prompt_values(h):
                p, e = h // 2, 64 * (h % 2)
                pe.wait_ge(sem("p_ready"), h + 1)
                if h >= 2:
                    pe.wait_ge(sem("pT_ready"), h - 1)
                for j in range(3):
                    last = pe.transpose(ps[2 + h % 2][:, P * j:P * j + P], sc[:, h % 2, P * j:P * j + P], ident)
                last.then_inc(sem("pT_ps"), 1)
                pe.wait_ge(sem("pT_ready"), h + 1)
                if h >= 4 and h % 2 == 0:
                    pe.wait_ge(sem("ppv_ev"), p - 1)
                o = ps[4 + p % 2]
                mm(o[e:e + 64, 0:128], vtok[:, 0, 64 * h:64 * h + 64], pT[:, h % 2, 0:128], start=True, stop=True)
                group(o[e:e + 64, 128:256], [(vtok[:, j, 64 * h:64 * h + 64], pT[:, h % 2, P + P * j:2 * P + P * j])
                                             for j in range(2)]).then_inc(sem("ppv_ps"), 1)

            for h in range(HEADS + 1):
                if h < HEADS:
                    prompt_scores(h)
                if h >= 1:
                    prompt_values(h - 1)

            def sample_scores(s):
                if s == 0:
                    pe.wait_ge(sem("qx_ready"), 1)
                    pe.wait_ge(sem("pmask_done"), HEADS)
                if s >= 2:
                    pe.wait_ge(sem("smask_done"), s - 1)
                for e in range(2):
                    pe.wait_ge(sem(f"past_in{e}"), 64 * (s + 1))
                    o = ps[s % 2][64 * e:64 * e + 64, :]
                    group(o[:, 0:256].rearrange("p (g n) -> p g n", g=2),
                          [(QX[:, p, 2 * s + e, :], KV[:, e, 0, :, P * p:P * p + P]) for p in range(PAIRS)])
                    last = group(o[:, 256:320], [(QX[:, p, 2 * s + e, :], kTn[:, p, 256:320]) for p in range(PAIRS)])
                last.then_inc(sem("sscore_ps"), 1)

            def sample_values(s):
                pe.wait_ge(sem("s_ready"), s + 1)
                if s == 0:
                    pe.wait_ge(sem("pT_ready"), HEADS)
                    pe.wait_ge(sem("ppv_ev"), PAIRS)
                if s >= 2:
                    pe.wait_ge(sem("sT_ready"), s - 1)
                for j in range(2):
                    pe.transpose(ps[2 + s % 2][:, P * j:P * j + P], sc[:, s % 2, P * j:P * j + P], ident)
                pe.transpose(ps[2 + s % 2][0:64, 256:384], sc[:, s % 2, 256:320], ident).then_inc(sem("sT_ps"), 1)
                pe.wait_ge(sem("sT_ready"), s + 1)
                if s >= 2:
                    pe.wait_ge(sem("spv_ev"), s - 1)
                for e in range(2):
                    for p in range(PAIRS):
                        c = 64 * e + 16 * p
                        last = group(ps[4 + s % 2][:, c:c + 16],
                                     [(KV[:, e, 1, g, P * p:P * p + P], pT[:, s % 2, P * g + c:P * g + c + 16])
                                      for g in range(2)]
                                     + [(vtok[0:64, 2, P * p:P * p + P], pT[0:64, s % 2, 256 + c:256 + c + 16])])
                    last.then_inc(sem("spv_used"), 1)

            for s in range(4):
                sample_scores(s)
                sample_values(s)

            def project_out(at, src, name):
                for i in range(2):
                    project(at + i, src, name, 4 * i)

            pe.wait_ge(sem("spv_ev"), 4)
            project_out(AT_EVEN_OUT, mixT, "res0")

            def router(l):
                pe.wait_ge(sem("u_ready"), 2 * l + 2)
                if l == 0:
                    pe.wait_ge(sem("rw_in"), 16)
                    pe.wait_ge(sem("rb_in"), 16)
                for t, rows in enumerate(TROWS):
                    last = group(ps[5][0:rows, 20 * t:20 * t + 20],
                                 [(uT[:, k, P * t:P * t + rows], rw[:, l, k, :]) for k in range(DT)]
                                 + [(ones[0:1, 0:rows], rb[0:1, l, :])])
                last.then_inc(sem("logits_ps"), 1)

            def experts(l):
                def expert(n, it=None):
                    at = AT_MOE[l] + 3 * n
                    r3 = None if it is None else it * 3

                    def k(v, per):
                        return v if it is None else it * (4 * per) + v
                    pe.wait_ge(sem(f"cdiag_ready{l}"), k(n + 1, 1))
                    for t, rows in enumerate(TROWS):
                        last = mm(ps[7][:, P * t:P * t + rows], ones[0:rows, :], cdiag[0:rows, t, 0:rows],
                                  start=True, stop=True)
                    last.then_inc(sem(f"cb_ps{l}"), 1)
                    piece(at, r3)
                    piece(at + 1, r3)
                    for f in range(FT):
                        g = FT * n + f
                        if it is not None or g >= 2:
                            pe.wait_ge(sem(f"h13_used{l}"), k(g - 1, FT))
                        for i in range(2):
                            w = w8[(at + i) % RING]
                            last = group(ps[2 * (f % 2) + i][:, 0:T],
                                         [(w[:, kk, P * f:P * f + P], uT[:, kk, :]) for kk in range(DT)])
                            if f == FT - 1:
                                used(at + i)
                        last.then_inc(sem(f"h13_ready{l}"), 1)
                    piece(at + 2, r3)
                    pe.wait_ge(sem(f"act_ready{l}"), k(FT * (n + 1), FT))
                    for m in range(DT):
                        g = DT * n + m
                        if it is not None or g >= 3:
                            pe.wait_ge(sem(f"y_ev{l}"), k(g - 2, DT))
                        last = group(ps[4 + m % 3][:, 0:T],
                                     [(w4[(at + 2) % RING][:, f, P * m:P * m + P], act[:, n % 2, f, :]) for f in range(FT)])
                        last.then_inc(sem(f"y_ps{l}"), 1)
                    used(at + 2)
                for n in range(4):
                    expert(n)
                with pe.Fori(1, 4) as it:
                    for n in range(4):
                        expert(n, it)

            norm(1)
            router(0)
            experts(0)
            norm(2)
            pe.wait_ge(sem("u_ready"), 3)
            for i in range(4):
                project(AT_ODD + i, uT, "odd", 4 * i)
            pe.wait_ge(sem("conv_ready"), 1)
            piece(AT_LRU)
            wl = ring[AT_LRU % RING][:, :].rearrange("p (g h k n) -> p g h k n", g=2, h=4, k=2)
            for m in range(16):
                g, h, j = m // 8, m % 8 // 2, m % 2
                if m >= 4:
                    pe.wait_ge(sem("lru_ev"), m - 3)
                last = group(ps[m % 4][:, 0:T], [(wl[:, g, h, k, P * j:P * j + P], xc[:, 2 * h + k, :]) for k in range(2)])
                last.then_inc(sem("lru_ready"), 1)
            used(AT_LRU)
            pe.wait_ge(sem("odd_mix_ready"), 1)
            project_out(AT_ODD_OUT, xc, "res1")
            norm(3)
            router(1)
            experts(1)
            norm(4)
            assert not gone

        @block.vector
        def _(v):
            step = Chain(v, sem("v_step"))
            tt, ts, stt, cp = v.tensor_tensor, v.tensor_scalar, v.scalar_tensor_tensor, v.tensor_copy
            MUL, ADD, SUB, MAX, MIN, EQ, GE = ALU.mult, ALU.add, ALU.subtract, ALU.max, ALU.min, ALU.is_equal, ALU.is_ge

            def over(ap, n, axis=2):
                s = list(ap.shape)
                return ap.unsqueeze(axis).broadcast_to(s[:axis] + [n] + s[axis:])

            def bt(x):
                return x.rearrange("p (b t) -> p b t", t=S_LEN)

            def bt3(x):
                return x.rearrange("p m (b t) -> p m b t", t=S_LEN)

            def norm(n):
                v.wait_ge(sem("rms_ready"), 2 * n + 2)
                step(v.reciprocal(stat[:, 4:6], stat[:, 0:2]))
                step(v.reciprocal(stat[0:64, 6:7], stat[0:64, 2:3]))
                for t, rows in enumerate(TROWS):
                    last = ts(diag[0:rows, t, :], ident[0:rows, :], stat[0:rows, 4 + t:5 + t], None, MUL)
                last.then_inc(sem("rdiag_ready"), 1)
                v.wait_ge(sem("rstd_ready"), n + 1)
                step(tt(tmp[:, :, :], hT[:, :, :], over(ps[6][:, 0:T], DT, 1), MUL))
                if n == 4:
                    for m in range(DT):
                        last = ts(uT[:, m, :], tmp[:, m, :], cols[:, C_NFIN + m:C_NFIN + m + 1], None, MUL)
                    last.then_inc(sem("y_ready"), 1)
                    return
                for m in range(DT):
                    ts(uT[:, m, 0:NP_TOK], tmp[:, m, 0:NP_TOK], gain[:, n, m, 0:1], shift(n)[:, m, 0:1], MUL, ADD)
                step(tt(bt3(uT[:, :, NP_TOK:T]), bt3(tmp[:, :, NP_TOK:T]), over(gain[:, n, :, 1:NSEQ], S_LEN, 3), MUL))
                tt(bt3(uT[:, :, NP_TOK:T]), bt3(uT[:, :, NP_TOK:T]), over(shift(n)[:, :, 1:NSEQ], S_LEN, 3), ADD)\
                    .then_inc(sem("u_ready"), 1)

            def residual(n, name):
                for m in range(DT):
                    v.wait_ge(sem(f"{name}_ps"), m + 1)
                    src = ps[m % 4]
                    step(tt(bt(sadd[:, m % 2, :]), bt(src[:, NP_TOK:T]), over(gate(n)[:, m, 1:NSEQ], S_LEN), MUL))
                    stt(hT[:, m, 0:NP_TOK], src[:, 0:NP_TOK], gate(n)[:, m, 0:1], hT[:, m, 0:NP_TOK], MUL, ADD)\
                        .then_inc(sem(f"{name}_ev"), 1)
                    last = tt(hT[:, m, NP_TOK:T], hT[:, m, NP_TOK:T], sadd[:, m % 2, :], ADD)
                last.then_inc(sem("h_ready"), 1)

            def top1(src, m, eq, c, oh):
                step(v.tensor_reduce(rt[:, :, m:m + 1], src, AX, MAX))
                step(tt(rt[:, :, eq:eq + 4], src, rt[:, :, m:m + 1].broadcast_to([P, TT, 4]), GE))
                step(tt(rt[:, :, eq:eq + 4], rt[:, :, eq:eq + 4], over(const[:, K_RANK:K_RANK + 4], TT, 1), MUL))
                step(v.tensor_reduce(rt[:, :, c:c + 1], rt[:, :, eq:eq + 4], AX, MAX))
                step(tt(rt[:, :, oh:oh + 4], rt[:, :, eq:eq + 4], rt[:, :, c:c + 1].broadcast_to([P, TT, 4]), EQ))

            def router(l):
                if l == 0:
                    v.wait_ge(sem("kv_stored"), 64)
                step(v.memset(lg, 0.0))
                v.wait_ge(sem("logits_ps"), l + 1)
                cp(lg[:, 0:2, :], ps[5][:, 0:40].rearrange("p (t n) -> p t n", t=2))
                step(cp(lg[0:64, 2, :], ps[5][0:64, 40:60]))
                top1(lg[:, :, 0:4], 8, 12, 16, 20)
                tt(rt[:, :, 0:4], lg[:, :, 0:4], rt[:, :, 8:9].broadcast_to([P, TT, 4]), SUB).then_inc(sem("rexp_in"), 1)
                for g in range(GROUPS):
                    last = tt(rt[:, :, 24 + 4 * g:28 + 4 * g], lg[:, :, 4 + 4 * g:8 + 4 * g],
                              rt[:, :, 20 + g:21 + g].broadcast_to([P, TT, 4]), MUL)
                step(last)
                step(tt(rt[:, :, 24:32], rt[:, :, 24:32], rt[:, :, 32:40], ADD))
                step(tt(rt[:, :, 44:48], rt[:, :, 24:28], rt[:, :, 28:32], ADD))
                top1(rt[:, :, 44:48], 48, 12, 16, 52)
                step(stt(rt[:, :, 56:60], rt[:, :, 52:56], FAR, rt[:, :, 44:48], MUL, ADD))
                top1(rt[:, :, 56:60], 60, 12, 16, 64)
                tt(rt[:, :, 40:41], rt[:, :, 60:61], rt[:, :, 48:49], SUB).then_inc(sem("rexp_in"), 1)
                v.wait_ge(sem("rexp_out"), 2 * l + 2)
                step(v.tensor_reduce(rt[:, :, 9:10], rt[:, :, 4:8], AX, ADD))
                step(ts(rt[:, :, 10:11], rt[:, :, 41:42], 1.0, None, ADD))
                step(tt(rt[:, :, 10:11], rt[:, :, 10:11], rt[:, :, 9:10], MUL))
                step(v.reciprocal(rt[:, :, 68:69], rt[:, :, 10:11]))
                step(tt(rt[:, :, 69:70], rt[:, :, 68:69], rt[:, :, 41:42], MUL))
                tt(rt[:, :, 52:56], rt[:, :, 52:56], rt[:, :, 68:69].broadcast_to([P, TT, 4]), MUL)
                step(tt(rt[:, :, 64:68], rt[:, :, 64:68], rt[:, :, 69:70].broadcast_to([P, TT, 4]), MUL))
                step(tt(rt[:, :, 72:76], rt[:, :, 52:56], rt[:, :, 64:68], ADD))
                for g in range(GROUPS):
                    last = tt(comb[:, :, 4 * g:4 * g + 4], rt[:, :, 72:76],
                              rt[:, :, 20 + g:21 + g].broadcast_to([P, TT, 4]), MUL)
                step(last)

            def experts(l):
                step(v.memset(yacc, 0.0))

                def expert(n, it=None):
                    def k(x, per):
                        return x if it is None else it * (4 * per) + x
                    if it is not None or n >= 1:
                        v.wait_ge(sem(f"cb_ps{l}"), k(n, 1))
                    for t, rows in enumerate(TROWS):
                        c = comb[0:rows, t, n:n + 1] if it is None else comb[0:rows, t, bass.ds(it * 4 + n, 1)]
                        last = ts(cdiag[0:rows, t, :], ident[0:rows, :], c, None, MUL)
                    last.then_inc(sem(f"cdiag_ready{l}"), 1)
                    v.wait_ge(sem(f"cb_ps{l}"), k(n + 1, 1))
                    step(cp(cb[:, n % 2, :], ps[7][:, 0:T]))
                    for f in range(FT):
                        v.wait_ge(sem(f"sig_ready{l}"), k(FT * n + f + 1, FT))
                        s, h1, h3 = sig[:, f % 2, :], ps[2 * (f % 2)][:, 0:T], ps[2 * (f % 2) + 1][:, 0:T]
                        a = act[:, n % 2, f, :]
                        step(tt(a, s, h1, MUL))
                        tt(a, a, h3, MUL).then_inc(sem(f"h13_used{l}"), 1)
                        v.wait_ge(sem(f"h13_used{l}"), k(FT * n + f + 1, FT))
                        tt(a, a, cb[:, n % 2, :], MUL).then_inc(sem(f"act_ready{l}"), 1)
                    for m in range(DT):
                        v.wait_ge(sem(f"y_ps{l}"), k(DT * n + m + 1, DT))
                        tt(yacc[:, m, :], yacc[:, m, :], ps[4 + m % 3][:, 0:T], ADD).then_inc(sem(f"y_ev{l}"), 1)
                    v.wait_ge(sem(f"y_ev{l}"), k(DT * (n + 1), DT))
                for n in range(4):
                    expert(n)
                with v.Fori(1, 4) as it:
                    step.enter(it - 1, 4 * (1 + FT))
                    for n in range(4):
                        expert(n, it)
                    step.leave(3)
                n = 2 * l + 1
                for m in range(DT):
                    stt(hT[:, m, 0:NP_TOK], yacc[:, m, 0:NP_TOK], gate(n)[:, m, 0:1], hT[:, m, 0:NP_TOK], MUL, ADD)
                step(tt(bt3(yacc[:, :, NP_TOK:T]), bt3(yacc[:, :, NP_TOK:T]), over(gate(n)[:, :, 1:NSEQ], S_LEN, 3), MUL))
                tt(hT[:, :, NP_TOK:T], hT[:, :, NP_TOK:T], yacc[:, :, NP_TOK:T], ADD).then_inc(sem("h_ready"), 1)

            v.wait_ge(sem("cols_in"), 16)
            v.wait_ge(sem("const_in"), 16)
            tt(stat[:, 12:16], cols[:, C_LB:C_LB + 4], cols[:, C_LB + 4:C_LB + 8], SUB).then_inc(sem("lb_in"), 1)
            v.wait_ge(sem(f"piece_used{RING - 1}"), 2 * ADA_PIECES // RING)
            for l in range(2):
                last = tt(mods[:, l, :, :], ps[l][:, 0:48 * NSEQ].rearrange("p (m b) -> p m b", b=NSEQ),
                          over(adab(l), NSEQ), ADD)
            step(last)
            for n in range(4):
                l, w = n // 2, n % 2
                c = (C_NMIX, C_NFFN)[w] + 8 * l
                stt(gain[:, n, :, :], mods[:, l, 24 * w + 8:24 * w + 16, :], 1.0, over(cols[:, c:c + 8], NSEQ), ADD, MUL)
            norm(0)
            for n in range(16):
                v.wait_ge(sem("prj_ps"), n + 1)
                cp(prj[:, n, :], ps[n % 4][:, 0:T]).then_inc(sem("prj_ev"), 1)
            v.wait_ge(sem("lb_ready"), 1)
            v.wait_ge(sem("hsig_ready"), 3)
            v.wait_ge(sem("prj_ev"), 16)
            step(ts(stat[:, 28:32], stat[:, 8:12], -1.0, 1.0, MUL, ADD))
            tt(prj[:, 0:4, :], prj[:, 0:4, :], xlag, MUL)
            tt(prj[:, 12:16, :], prj[:, 12:16, :], wlag[0], MUL)
            for h in range(HG):
                last = ts(prj[:, 4 + h, :], tlag[:, h, :], stat[:, 28 + h:29 + h], stat[:, 8 + h:9 + h], MUL, ADD)
            step(last)
            q_, f_, v_ = prj[:, 0:4, :], prj[:, 4:8, :], prj[:, 8:12, :]

            def c8(x):
                return x.rearrange("p h (c t) -> p (h c) t", t=CH)

            def lag_out(d):
                v.wait_ge(sem("lag_ps"), d + 1)
                s = banks[:, 4 * (d % 2):4 * (d % 2) + 4, 0:NCHUNK * (CH - d)].rearrange("p h (c t) -> p h c t", t=CH - d)
                vals = v_.rearrange("p h (c t) -> p h c t", t=CH)[:, :, :, 0:CH - d]
                dst = (oB if d == 0 else tlag).rearrange("p h (c t) -> p h c t", t=CH)[:, :, :, d:CH]
                last = tt(dst, s, vals, MUL)
                last.then_inc(sem("lag_ev"), 1)
                v.wait_ge(sem("lag_ev"), d + 1)
                if d:
                    step(tt(c8(oB)[:, :, d:CH], c8(oB)[:, :, d:CH], c8(tlag)[:, :, d:CH], ADD))

            step(ts(kf, f_, -1.0, 1.0, MUL, ADD))
            for d in range(CH):
                X, W, W0 = (xlag, xlag2)[d % 2], wlag[d % 2], (wlag[(d + 1) % 2] if d > 1 else kf)
                if d >= 2:
                    v.wait_ge(sem("lag_ps"), d - 1)
                if d == 0:
                    tt(X, q_, kf, MUL).then_inc(sem("xlag_ready"), 1)
                else:
                    step(tt(c8(W)[:, :, d:CH], c8(f_)[:, :, d:CH], c8(W0)[:, :, d - 1:CH - 1], MUL))
                    tt(c8(X)[:, :, d:CH], c8(q_)[:, :, d:CH], c8(W)[:, :, d:CH], MUL).then_inc(sem("xlag_ready"), 1)
                if d >= 1:
                    lag_out(d - 1)
            lag_out(CH - 1)

            cp(c8(pre)[:, :, 0:1], c8(f_)[:, :, 0:1])
            step(v.memset(c8(suf)[:, :, CH - 1:CH], 1.0))
            for i in range(1, CH):
                j = CH - 1 - i
                tt(c8(pre)[:, :, i:i + 1], c8(pre)[:, :, i - 1:i], c8(f_)[:, :, i:i + 1], MUL)
                step(tt(c8(suf)[:, :, j:j + 1], c8(suf)[:, :, j + 1:j + 2], c8(f_)[:, :, j + 1:j + 2], MUL))
            tt(suf, suf, kf, MUL)
            tt(q_, q_, pre, MUL)
            for h in range(HG):
                last = v.memset(S_ST[:, 0, h, :], 0.0)
            last.then_inc(sem("ktil_ready"), 1)
            v.wait_ge(sem("ktil_ready"), 1)
            v.wait_ge(sem("s0_in"), 16)

            def turn(t):
                rows = TROWS[t]
                v.wait_ge(sem("turn_ps"), 2 * t + 1)
                cp(ktok[0:rows, t % 2, :], ps[7][0:rows, :]).then_inc(sem("turn_ev"), 1)
                v.wait_ge(sem("turn_ps"), 2 * t + 2)
                for c in range(4):
                    last = ts(vexp[0:rows, t % 2, c, :], ps[7][0:rows, :], const[0:rows, K_CM + c:K_CM + c + 1], None, MUL)
                last.then_inc(sem("turn_ev"), 1)

            def chain(G):
                for half in range(2):
                    u = 2 * G + half
                    v.wait_ge(sem("upd_ps"), u + 1)
                    for c in (2 * half, 2 * half + 1):
                        j = 4 * G + c
                        if G < 8:
                            if c == 3 and G >= 1:
                                v.wait_ge(sem("inter_ps"), G)
                            elif G >= 2:
                                v.wait_ge(sem("inter_ps"), G - 1)
                        elif c == 0:
                            v.wait_ge(sem("inter_ps"), G + 1)
                        for h in range(HG):
                            S = S_ST[:, j % 8, h, :] if G < 8 else S_END[:, j - 31, h, :]
                            So = (S_END[:, 0, h, :] if j == 31 else S_ST[:, (j + 1) % 8, h, :]) if G < 8 else S
                            U = ps[2 * (u % 3) + h // 2][:, 256 * (h % 2) + P * (c % 2):256 * (h % 2) + P * (c % 2) + P]
                            last = stt(So, S, pre[:, h, 8 * j + 7:8 * j + 8], U, MUL, ADD)
                        if c % 2 == 0:
                            step(last)
                    last.then_inc(sem("chain"), 1)
                    v.wait_ge(sem("chain"), u + 1)

            def inter(G):
                v.wait_ge(sem("inter_ps"), G + 1)
                tt(oB[:, :, 32 * G:32 * G + 32], oB[:, :, 32 * G:32 * G + 32],
                   ps[6][:, 0:128].rearrange("p (h n) -> p h n", h=HG), ADD).then_inc(sem("inter_ev"), 1)

            turn(0)
            for G in range(8):
                chain(G)
                if G % 4 == 1:
                    turn(G // 4 + 1)
                inter(G)
            inter(8)
            chain(8)
            inter(9)
            chain(9)
            v.wait_ge(sem("orms_ready"), 2)
            step(v.reciprocal(stat[:, 32:40], stat[:, 16:24]))
            step(v.reciprocal(stat[0:64, 40:44], stat[0:64, 24:28]))
            for t, rows in enumerate(TROWS):
                for h in range(HG):
                    c = 32 + 4 * t + h
                    last = ts(odiag[0:rows, t, h, :], ident[0:rows, :], stat[0:rows, c:c + 1], None, MUL)
            last.then_inc(sem("odiag_ready"), 1)
            v.wait_ge(sem("orstd_ready"), 1)
            step(stt(tlag, oB, cols[:, C_HGW:C_HGW + 1], banks[:, 0:4, 0:T], MUL, MUL))
            tt(mixT[:, 4:8, :], tlag, prj[:, 12:16, :], MUL).then_inc(sem("hgrn_done"), 1)
            v.wait_ge(sem("hgrn_done"), 1)

            v.memset(QX, 0.0)
            for n in range(9):
                t, rows = n % 3, TROWS[n % 3]
                v.wait_ge(sem("qkv_ps"), n + 1)
                src = ps[n % 6][0:rows, :]
                if n >= 6:
                    cp(vtok[0:rows, t, :], src).then_inc(sem("qkv_ev"), 1)
                    continue
                x = src.rearrange("p (h d) -> p h d", d=DH)
                a = rt1[0:rows, :].rearrange("p (h d) -> p h d", d=DH)
                b = rt2[0:rows, :].rearrange("p (h d) -> p h d", d=DH)
                cos = const[0:rows, K_COS + DH * t:K_COS + DH * t + DH]
                sin = const[0:rows, K_SIN + DH * t:K_SIN + DH * t + DH]
                tt(a, x, over(cos, HEADS, 1), MUL)
                tt(b[:, :, 0:32], x[:, :, 32:64], over(sin[:, 0:32], HEADS, 1), MUL)
                step(tt(b[:, :, 32:64], x[:, :, 0:32], over(sin[:, 32:64], HEADS, 1), MUL))
                dst = (qtok, ktk)[n // 3][0:rows, t, :]
                tt(dst, rt1[0:rows, :], rt2[0:rows, :], ADD).then_inc(sem("qkv_ev"), 1)
                v.wait_ge(sem("qkv_ev"), n + 1)
            for n in range(9, 15):
                w, t = (n - 9) // 3, n % 3
                rows = TROWS[t]
                v.wait_ge(sem("qkv_ps"), n + 1)
                cp(qkT[:, w, :, P * t:P * t + rows], ps[n % 6][:, :].rearrange("p (a n) -> p a n", a=4)[:, :, 0:rows])\
                    .then_inc(sem("qkv_ev"), 1)
            v.wait_ge(sem("qkv_ev"), 15)
            for p in range(PAIRS):
                for e in range(2):
                    last = cp(QX[64 * e:64 * e + 64, p, :, 16 * p + 8 * e:16 * p + 8 * e + 8],
                              bt(qkT[64 * e:64 * e + 64, 0, p, NP_TOK:T]))
            last.then_inc(sem("qx_ready"), 1)

            def prompt_front(h):
                s = sm[:, h % 2, :]
                v.wait_ge(sem("pscore_ps"), h + 1)
                x = sc[:, h % 2, :]
                stt(x, ps[h % 2][:, 0:384], SCALE, const[:, K_MP:K_MP + 384], MUL, ADD).then_inc(sem("pmask_done"), 1)
                v.wait_ge(sem("pmask_done"), h + 1)
                v.tensor_reduce(s[:, 2:3], x[:, 0:128], AX, MAX)
                step(v.tensor_reduce(s[:, 3:4], x[:, 128:384], AX, MAX))
                ts(s[:, 0:2], s[:, 2:4], -1.0, None, MUL).then_inc(sem("pmax_ready"), 1)

            def prompt_back(h):
                s, x = sm[:, h % 2, :], sc[:, h % 2, :]
                v.wait_ge(sem("pexp_ready"), 2 * h + 2)
                step(v.reciprocal(s[:, 6:8], s[:, 4:6]))
                ts(x[:, 0:128], x[:, 0:128], s[:, 6:7], None, MUL)
                ts(x[:, 128:384], x[:, 128:384], s[:, 7:8], None, MUL).then_inc(sem("p_ready"), 1)
                v.wait_ge(sem("pT_ps"), h + 1)
                if h >= 2:
                    v.wait_ge(sem("ppv_ps"), h - 1)
                cp(pT[:, h % 2, :], ps[2 + h % 2][:, 0:384]).then_inc(sem("pT_ready"), 1)
                if h % 2:
                    v.wait_ge(sem("ppv_ps"), h + 1)
                    cp(mixT[:, h // 2, 0:NP_TOK], ps[4 + h // 2 % 2][:, 0:NP_TOK]).then_inc(sem("ppv_ev"), 1)

            for h in range(HEADS + 1):
                if h < HEADS:
                    prompt_front(h)
                if h >= 1:
                    prompt_back(h - 1)

            for s in range(4):
                m, x = sm[:, s % 2, :], sc[:, s % 2, 0:320]
                v.wait_ge(sem("sscore_ps"), s + 1)
                ts(x[:, 0:256], ps[s % 2][:, 0:256], SCALE, None, MUL)
                stt(x[:, 256:320], ps[s % 2][:, 256:320], SCALE, const[:, K_MS + 64 * s:K_MS + 64 * s + 64], MUL, ADD)\
                    .then_inc(sem("smask_done"), 1)
                v.wait_ge(sem("smask_done"), s + 1)
                step(v.tensor_reduce(m[:, 2:3], x, AX, MAX))
                ts(m[:, 0:1], m[:, 2:3], -1.0, None, MUL).then_inc(sem("smax_ready"), 1)
                v.wait_ge(sem("sexp_ready"), s + 1)
                step(v.reciprocal(m[:, 6:7], m[:, 4:5]))
                ts(x, x, m[:, 6:7], None, MUL).then_inc(sem("s_ready"), 1)
                v.wait_ge(sem("sT_ps"), s + 1)
                cp(pT[:, s % 2, 0:256], ps[2 + s % 2][:, 0:256])
                cp(pT[0:64, s % 2, 256:384], ps[2 + s % 2][0:64, 256:384]).then_inc(sem("sT_ready"), 1)
                v.wait_ge(sem("spv_used"), 2 * s + 2)
                for e in range(2):
                    o = mixT[64 * e:64 * e + 64, 0:4, NP_TOK + 16 * s:NP_TOK + 16 * s + 16]\
                        .rearrange("p m (b t) -> p b m t", t=S_LEN)
                    i = ps[4 + s % 2][64 * e:64 * e + 64, 0:128].rearrange("p (b m n) -> p b m n", b=2, m=4)
                    last = cp(o, i[:, :, :, 8 * e:8 * e + 8])
                last.then_inc(sem("spv_ev"), 1)
            residual(0, "res0")
            norm(1)
            router(0)
            experts(0)
            norm(2)

            v.wait_ge(sem("hist_in"), 32)
            v.wait_ge(sem("hgrn_stored"), 16)
            v.memset(recP[:, :, 0:3], 0.0)
            cp(recS[:, :, :, 0:3], hist)
            for n in range(16):
                v.wait_ge(sem("odd_ps"), n + 1)
                src, m = ps[n % 4], n % 8
                if n < 8:
                    cp(gT[:, m, :], src[:, 0:T]).then_inc(sem("odd_ev"), 1)
                else:
                    cp(recP[:, m, 3:3 + NP_TOK], src[:, 0:NP_TOK])
                    cp(recS[:, m, :, 3:3 + S_LEN], bt(src[:, NP_TOK:T])).then_inc(sem("odd_ev"), 1)
                if n == 7:
                    v.wait_ge(sem("odd_ev"), 8)
                    c = float(np.sqrt(2.0 / np.pi))
                    step(tt(t1, gT, gT, MUL))
                    step(ts(t1, t1, 0.044715 * c, c, MUL, ADD))
                    tt(t1, t1, gT, MUL).then_inc(sem("gelu_in"), 1)
                if n == 11:
                    v.wait_ge(sem("gelu_out"), 1)
                    stt(gT, t1, 1.0, gT, ADD, MUL)
            v.wait_ge(sem("odd_ev"), 16)
            for j in range(CONV):
                for m in range(DT):
                    w = cols[:, C_CONVW + 8 * j + m:C_CONVW + 8 * j + m + 1]
                    xp, xs = xc[:, m, 0:NP_TOK], bt(xc[:, m, NP_TOK:T])
                    rp, rs = recP[:, m, j:j + NP_TOK], recS[:, m, :, j:j + S_LEN]
                    if j == 0:
                        b = cols[:, C_CONVB + m:C_CONVB + m + 1]
                        ts(xp, rp, w, b, MUL, ADD)
                        last = ts(xs, rs, w, b, MUL, ADD)
                    else:
                        stt(xp, rp, w, xp, MUL, ADD)
                        last = stt(xs, rs, w, xs, MUL, ADD)
                if j < CONV - 1:
                    step(last)
            last.then_inc(sem("conv_ready"), 1)
            cp(cst[:, :, 0, :], recP[:, :, NP_TOK:NP_TOK + 3])
            cp(cst[:, :, 1:NSEQ, :], recS[:, :, :, S_LEN:S_LEN + 3])
            L = [lsp[:, i, :] for i in range(6)]
            step(ts(L[2], cols[:, C_LAM:C_LAM + DT], -1.0, None, MUL))
            tt(L[0], L[2], cols[:, C_LAM:C_LAM + DT], MAX).then_inc(sem("lam_in"), 1)
            v.wait_ge(sem("lam_out"), 1)
            step(ts(L[3], L[1], 2.0, None, ADD))
            step(v.reciprocal(L[3], L[3]))
            step(tt(L[3], L[3], L[1], MUL))
            step(tt(L[4], L[3], L[3], MUL))
            step(ts(L[5], L[4], 1.0 / 17, 1.0 / 15, MUL, ADD))
            for k in range(13, 0, -2):
                step(tt(L[5], L[5], L[4], MUL))
                step(ts(L[5], L[5], 1.0 / k, None, ADD))
            step(tt(L[5], L[5], L[3], MUL))
            step(ts(L[2], L[2], 0.0, None, MAX))
            step(stt(L[5], L[5], 2.0, L[2], MUL, ADD))
            step(ts(L[5], L[5], -8.0, None, MUL))
            v.wait_ge(sem("lru_ev"), 16)
            tt(rT, rT, over(L[5], T), MUL).then_inc(sem("loga_ready"), 1)
            step(tt(iT, iT, xc, MUL))
            v.wait_ge(sem("a_ready"), 2)
            step(tt(hs, aT, aT, MUL))
            stt(t1, hs, 1.0, t1, ADD, MUL).then_inc(sem("om_ready"), 1)
            v.wait_ge(sem("root_ready"), 1)
            step(tt(t1, t1, iT, MUL))
            a0 = bt3(aT[:, :, NP_TOK:T])[:, :, :, 0]
            x0 = bt3(t1[:, :, NP_TOK:T])[:, :, :, 0]
            step(tt(lru0, lru0, a0, MUL))
            tt(x0, x0, lru0, ADD)
            v.memset(aT[:, :, 0:1], 0.0)
            step(v.memset(bt3(aT[:, :, NP_TOK:T])[:, :, :, 0:1], 0.0))
            step(v.tensor_tensor_scan(hs.rearrange("p m t -> p (m t)"), aT.rearrange("p m t -> p (m t)"),
                                      t1.rearrange("p m t -> p (m t)"), 0.0, MUL, ADD))
            cp(ends[:, :, 0:1], hs[:, :, NP_TOK - 1:NP_TOK])
            cp(ends[:, :, 1:NSEQ], bt3(hs[:, :, NP_TOK:T])[:, :, :, S_LEN - 1]).then_inc(sem("ends_ready"), 1)
            stt(xc, hs, 0.5, gT, MUL, MUL).then_inc(sem("odd_mix_ready"), 1)
            residual(2, "res1")
            norm(3)
            router(1)
            experts(1)
            norm(4)


_OUTS = {"yT": (P, DT, T), "k": (T, 512), "v": (T, 512), "hgrn": (P, NSEQ, HG, P),
         "convT": (P, DT, NSEQ, 3), "lruT": (P, DT, NSEQ)}


def shape_constants():
    f = np.float32
    K = np.zeros((P, N_CONST), f)
    K[:, K_ID:K_ID + P] = np.eye(P, dtype=f)
    half = DH // 2
    inv = np.power(f(10000.0), -np.arange(half, dtype=f) / f(half)).astype(f)
    pos = np.concatenate([np.arange(NP_TOK), np.tile(PAST_PAGES * PAGE + np.arange(S_LEN), NS_SEQ)]).astype(f)
    ang = np.zeros((TT * P, half), f)
    ang[:T] = pos[:, None] * inv[None, :]
    cos, sin = np.cos(ang).astype(f), np.sin(ang).astype(f)
    for t in range(TT):
        r = slice(P * t, P * t + P)
        K[:, K_COS + DH * t:K_COS + DH * t + DH] = np.concatenate([cos[r], cos[r]], 1)
        K[:, K_SIN + DH * t:K_SIN + DH * t + DH] = np.concatenate([-sin[r], sin[r]], 1)
    row, col = np.arange(P)[:, None], np.arange(2 * P)[None, :]
    K[:, K_MP:K_MP + 128] = np.where(col[:, :P] <= row, 0, FAR)
    K[:, K_MP + 128:K_MP + 384] = np.where(col <= row + P, 0, FAR)
    e, q = np.arange(P) // 64, np.arange(P) % 8
    for s in range(4):
        key = np.arange(64)[None, :]
        ok = (key // 8 == (2 * s + e)[:, None]) & (key % 8 <= q[:, None])
        K[:, K_MS + 64 * s:K_MS + 64 * s + 64] = np.where(ok, 0, FAR)
    for c in range(4):
        K[:, K_CM + c] = (np.arange(P) // CH % 4 == c)
    K[:, K_RANK:K_RANK + 4] = [4, 3, 2, 1]
    K[:, K_EPS] = EPS
    return K


def kernel(**a):
    import concourse.bacc as bacc
    from concourse.bass_utils import run_bass_kernel_spmd

    a = {k: np.asarray(x) for k, x in a.items()}

    def feat(x):
        return np.ascontiguousarray(x.reshape(x.shape[0], -1, P).transpose(2, 1, 0))

    def columns(x):
        return x.reshape(-1, P).T

    def pieces(w, n):
        k = w.shape[0] // P
        return w.reshape(k, P, -1, n).transpose(2, 1, 0, 3).reshape(-1, P, k * n)

    even = pieces(a["w_in_even"][0], 512)
    experts = [np.stack([pieces(a[w][l, e], n)[0] for e in range(NE)
                         for w, n in (("moe_w1", 512), ("moe_w3", 512), ("moe_w2", 1024))]) for l in range(2)]
    lru = np.stack([a["lru_wa"][0], a["lru_wx"][0]]).reshape(2, 4, 2, P, 256).transpose(3, 0, 1, 2, 4).reshape(1, P, PIECE)
    w = np.concatenate([pieces(a["ada_w"][0], 512), pieces(a["ada_w"][1], 512), even[3:7], even[0:3],
                        pieces(a["w_out_even"][0], 512), experts[0], pieces(a["w_in_odd"][0], 512), lru,
                        pieces(a["w_out_odd"][0], 512), experts[1]])
    x = np.concatenate([a["x_prompt"].reshape(-1, D), a["x_sample"].reshape(-1, D)])
    c = np.concatenate([a["c_prompt"], a["c_sample"]])
    cols = np.concatenate([columns(a[n]) for n in ("ada_b", "norm_mix", "norm_ffn", "norm_final", "hg_lower_bounds",
                                                   "hg_norm_w", "conv_w", "conv_b", "lru_ba", "lru_bx", "lru_lambda")], 1)
    rw = np.concatenate([a["router_group_w"], a["router_expert_w"]], 2).reshape(2, DT, P, 20).transpose(2, 0, 1, 3)
    rb = np.concatenate([a["router_group_b"], a["router_expert_b"]], 1)[None]
    n_phys = a["cache_k"].shape[1]
    kT = a["cache_k"][0].reshape(n_phys, PAGE, PAIRS, P).transpose(0, 3, 2, 1).reshape(n_phys, P, 512)
    arrays = {
        "w": w, "xT": feat(x), "cT": feat(c), "cols": cols, "const": shape_constants(), "rw": rw, "rb": rb,
        "kT": kT, "v": a["cache_v"][0].reshape(n_phys, PAGE, 512),
        "s0": a["state_hgrn"][0].transpose(2, 0, 1, 3),
        "convT": a["state_conv"][0].reshape(NS_SEQ, 3, DT, P).transpose(3, 2, 0, 1),
        "lruT": feat(a["state_lru"][0]),
        "pages": a["page_table"].reshape(1, -1),
    }
    nc = bacc.Bacc("TRN2", target_bir_lowering=False, num_devices=1)
    arrays = {f"in_{k}": np.ascontiguousarray(x) for k, x in arrays.items()}
    I = {k[3:]: nc.dram_tensor(k, x.shape, mybir.dt.from_np(x.dtype), kind="ExternalInput").ap() for k, x in arrays.items()}
    O = {k: nc.dram_tensor(f"out_{k}", s, F32, kind="ExternalOutput").ap() for k, s in _OUTS.items()}
    build(nc, I, O)
    r = run_bass_kernel_spmd(nc, [arrays], core_ids=[0]).results[0]
    y = r["out_yT"].transpose(2, 1, 0).reshape(T, D)
    kv = [r[f"out_{n}"] for n in "kv"]
    hg = r["out_hgrn"].transpose(1, 2, 0, 3)[None]
    conv = r["out_convT"].transpose(2, 3, 1, 0).reshape(1, NSEQ, 3, D)
    lru = r["out_lruT"].transpose(2, 1, 0).reshape(1, NSEQ, D)
    C = np.ascontiguousarray
    return (C(y[:NP_TOK].reshape(1, NP_TOK, D)), C(y[NP_TOK:].reshape(NS_SEQ, S_LEN, D)),
            *(C(x[:NP_TOK].reshape(1, 1, NP_TOK, HEADS, DH)) for x in kv),
            *(C(x[NP_TOK:].reshape(1, NS_SEQ, S_LEN, HEADS, DH)) for x in kv),
            C(hg[:, :1]), C(hg[:, 1:]), C(conv[:, :1]), C(conv[:, 1:]), C(lru[:, :1]), C(lru[:, 1:]))
```

```python
from contextlib import ExitStack

import numpy as np

import concourse.bass as bass
from concourse import mybir

P = 128
D = 1024
DT = D // P
NP_TOK, NS_SEQ, S_LEN = 256, 8, 8
NS_TOK = NS_SEQ * S_LEN
T = NP_TOK + NS_TOK
NSEQ = 1 + NS_SEQ
TT = 3
TROWS = (128, 128, 64)
HEADS, DH = 8, 64
PAIRS = HEADS // 2
HG = 4
CH = 8
NCHUNK = T // CH
PAGE = 128
PAST_PAGES = 2
GROUPS, EPG = 4, 4
NE = GROUPS * EPG
FF = 512
FT = FF // P
CONV = 4
N_PHYS = 20
EPS = 1e-6
SCALE = DH ** -0.5
FAR = -1e30

WIN = 72
SLOTS = 128
NOWHERE = 1000.0

PIECE = 4096
RING = 4
ADA_PIECES = 12
AT_ADA = 0
AT_EVEN = ADA_PIECES
AT_ADA1 = AT_EVEN + 4
AT_QKV = AT_ADA1 + ADA_PIECES
AT_EVEN_OUT = AT_QKV + 3
AT_MOE = (AT_EVEN_OUT + 2, AT_EVEN_OUT + 2 + 3 * NE + 7)
AT_ODD = AT_MOE[0] + 3 * NE
AT_LRU = AT_ODD + 4
AT_ODD_OUT = AT_LRU + 1
N_PIECES = AT_MOE[1] + 3 * NE
W1, W3, W2 = (0, 2, 5, 8), (1, 4, 7, 10), (3, 6, 9, 11)
assert AT_ODD_OUT + 2 == AT_MOE[1] and N_PIECES % RING == 0 and ADA_PIECES % RING == 0
ADA_BESIDE = (2, 1, 1, 1, 2, 1, 1, 1, 1, 1)

C_ADAB = 0
C_NMIX = C_ADAB + 96
C_NFFN = C_NMIX + 16
C_NFIN = C_NFFN + 16
C_LB = C_NFIN + 8
C_HGW = C_LB + 8
C_CONVW = C_HGW + 1
C_CONVB = C_CONVW + 32
C_BA = C_CONVB + 8
C_BX = C_BA + 8
C_LAM = C_BX + 8
N_COLS = C_LAM + 8

K_ID = 0
K_COS = K_ID + P
K_SIN = K_COS + TT * DH
K_MP = K_SIN + TT * DH
K_MS = K_MP + 384
K_CM = K_MS + 256
K_RANK = K_CM + 4
K_EPS = K_RANK + 4
K_TRI = K_EPS + 1
K_IOTA = K_TRI + P
K_SGN = K_IOTA + P
K_OFF = K_SGN + NE
N_CONST = K_OFF + NE

ALU = mybir.AluOpType
ACT = mybir.ActivationFunctionType
F32 = mybir.dt.float32
AX = mybir.AxisListType.X


class Chain:

    def __init__(self, eng, sem):
        self.eng, self.sem, self.n, self.it, self.per = eng, sem, 0, None, 0

    def enter(self, it, per):
        self.it, self.per, self.start = it, per, self.n

    def leave(self, trips):
        assert self.n - self.start == self.per, (self.n - self.start, self.per)
        self.n, self.it = self.start + self.per * trips, None

    def __call__(self, ins):
        ins.then_inc(self.sem, 1)
        self.n += 1
        self.eng.wait_ge(self.sem, self.n if self.it is None else self.it * self.per + self.n)


def build(nc, I, O):
    ctx = ExitStack()
    with ctx:
        sems = {}

        def sem(name):
            if name not in sems:
                sems[name] = ctx.enter_context(nc.semaphore(name))
            return sems[name]

        def sb(name, *shape, dt=F32):
            return ctx.enter_context(nc.sbuf_tensor(name, list(shape), dt))

        ring = [sb(f"ring{s}", P, PIECE) for s in range(RING)]
        w8 = [r[:, :].rearrange("p (k n) -> p k n", k=8) for r in ring]
        w4 = [r[:, :].rearrange("p (k n) -> p k n", k=4) for r in ring]
        hT = sb("hT", P, DT, T)
        uT = sb("uT", P, DT, T)
        tmp = sb("tmp", P, DT, T)
        const = sb("const", P, N_CONST)
        cols = sb("cols", P, N_COLS)
        ones = sb("ones", P, P)
        cT = sb("cT", P, DT, NSEQ)
        mods = sb("mods", P, 2, 48, NSEQ)
        gain = sb("gain", P, 4, DT, NSEQ)
        stat = sb("stat", P, 64)
        diag = sb("diag", P, TT, P)
        rw = sb("rw", P, 2, DT, 20)
        rb = sb("rb", 1, 2, 20)
        over_i = sb("over_i", 1, 1, dt=mybir.dt.int32)
        pages = sb("pages", 1, 2 * NS_SEQ, dt=mybir.dt.int32)
        SCR = 24064
        scr = sb("scr", P, SCR)
        banks = ctx.enter_context(nc.psum_tensor("banks", [P, 8, 512], F32))
        ps = [banks[:, b, :] for b in range(8)]
        sadd = sb("sadd", P, 2, NS_TOK)

        def carve(at, *shape):
            n = int(np.prod(shape))
            assert at + n <= SCR, (at, n)
            v = scr[:, at:at + n]
            if len(shape) == 1:
                return v
            names = "abcd"[:len(shape)]
            return v.rearrange(f"p ({' '.join(names)}) -> p {' '.join(names)}",
                               **{c: s for c, s in zip(names, shape)})

        ident = const[:, K_ID:K_ID + P]

        B = HG * T
        prj = carve(0, 16, T)
        kf = carve(4 * B, HG, T)
        pre = carve(5 * B, HG, T)
        suf = carve(6 * B, HG, T)
        wlag = [carve((7 + i) * B, HG, T) for i in range(2)]
        xlag = carve(9 * B, HG, T)
        tlag = carve(10 * B, HG, T)
        oB = carve(11 * B, HG, T)
        ktok = carve(7 * B, 2, 512)
        vexp = carve(7 * B + 1024, 2, 4, 512)
        S_END = carve(12 * B, NSEQ, HG, P)
        S_ST = carve(12 * B + NSEQ * 512, 8, HG, P)
        xlag2 = carve(12 * B + NSEQ * 512, HG, T)
        assert 7 * B + 1024 + 4096 <= 11 * B
        odiag = carve(7 * B, TT, HG, P)
        qtok = carve(0, TT, 512)
        ktk = carve(1536, TT, 512)
        vtok = carve(3072, TT, 512)
        qkT = carve(4608, 2, PAIRS, T)
        QX = carve(7168, PAIRS, NS_SEQ, 64)
        KV = [carve(at, 2, 2, 512) for at in (9216, 11264, 12 * B, 12 * B + 2048)]
        sc = carve(13312, 2, 384)
        pT = carve(14080, 2, 384)
        sm = carve(14848, 2, 8)
        assert 14912 <= 12 * B
        rt1 = carve(12 * B + NSEQ * 512, 512)
        rt2 = carve(12 * B + NSEQ * 512 + 512, 512)
        mixT = tmp
        mrow = tmp[0:NSEQ, 0:4, :].rearrange("p m t -> p (m t)")[:, 0:1024].rearrange("p (b n) -> p b n", b=2)

        gT = carve(0, DT, T)
        recP = carve(2560, DT, NP_TOK + 3)
        recS = carve(4632, DT, NS_SEQ, S_LEN + 3)
        hist = carve(21120, DT, NS_SEQ, 3)
        xc = carve(5336, DT, T)
        rT = carve(7896, DT, T)
        iT = carve(10456, DT, T)
        aT = carve(13016, DT, T)
        t1 = carve(15576, DT, T)
        hs = carve(18136, DT, T)
        lsp = carve(20696, 6, DT)
        lru0 = carve(20760, DT, NS_SEQ)
        ends = carve(20824, DT, NSEQ)
        cst = carve(20900, DT, NSEQ, 3)

        lg = carve(0, TT, 20)
        rt = carve(64, TT, 96)
        comb = carve(352, TT, NE + 4)
        slot = carve(412, TT, NE + 4)
        sel = carve(472, TT, NE)
        fits = carve(520, 16)
        yacc = carve(4840, DT, T)
        cdiag = carve(600, TT, P)
        cb = carve(1000, 2, T)
        sig = carve(1640, 2, T)
        act = carve(2280, 2, FT, T)
        pick = carve(600, TT, 4, WIN)
        spread = carve(1464, 2, TT, SLOTS)
        now = carve(2232, 2, TT, 4)
        back = carve(2256, T)
        sg = carve(2576, 2, FT, WIN)
        utok = carve(7400, TT, D)
        acts = carve(10472, 4, FT, SLOTS)
        xe = carve(12520, DT, 4, WIN)
        ye = carve(14824, 2, 512)

        def shift(s):
            l, w = s // 2, s % 2
            return mods[:, l, 24 * w:24 * w + 8, :]

        def gate(s):
            l, w = s // 2, s % 2
            return mods[:, l, 24 * w + 16:24 * w + 24, :]

        block = ctx.enter_context(nc.Block())

        @block.sync
        def _(sp):
            for s in range(RING):
                sp.dma_start(ring[s][:, :], I["w"][s, :, :]).then_inc(sem(f"piece_in{s}"), 16)
            with sp.Fori(1, N_PIECES // RING) as r:
                for s in range(RING):
                    sp.wait_ge(sem(f"piece_used{s}"), r)
                    sp.dma_start(ring[s][:, :], I["w"][r * RING + s, :, :]).then_inc(sem(f"piece_in{s}"), 16)

        @block.gpsimd
        def _(pool):
            pool.dma_start(pages[:, :], I["pages"]).then_inc(sem("pages_in"), 16)
            pool.memset(ones[:, :], 1.0).then_inc(sem("ones_ready"), 1)
            pool.wait_ge(sem("hgrn_done"), 1)
            pool.dma_start(O["hgrn"], S_END).then_inc(sem("hgrn_stored"), 16)
            pool.wait_ge(sem("pages_in"), 16)
            for b in range(NS_SEQ):
                if b == 2:
                    pool.wait_ge(sem("hgrn_stored"), 16)
                if b >= 4:
                    pool.wait_ge(sem("spv_used"), b - 3)
                for g in range(PAST_PAGES):
                    pg = pool.value_load(pages[0:1, 2 * b + g:2 * b + g + 1], min_val=0, max_val=N_PHYS - 1)
                    for i, src in enumerate((I["kT"], I["v"])):
                        pool.dma_start(KV[b % 4][:, i, g, :], src[bass.ds(pg, 1), :, :].rearrange("o p n -> p (o n)"))\
                            .then_inc(sem(f"past_in{b % 4}"), 16)
                if b == 3:
                    for n, (name, src) in enumerate((("k", ktk), ("v", vtok))):
                        pool.wait_ge(sem("qkv_ev"), 6 + 3 * n)
                        pool.dma_start(O[name][0:256, :].rearrange("(t p) n -> p t n", p=P), src[:, 0:2, :])\
                            .then_inc(sem("kv_stored"), 16)
                        pool.dma_start(O[name][256:T, :], src[0:64, 2, :]).then_inc(sem("kv_stored"), 16)

            def zero(l):
                pool.wait_ge(sem("u_ready"), 2 * l + 2)
                pool.memset(yacc, 0.0).then_inc(sem("zeroed"), 1)
                pool.memset(acts, 0.0).then_inc(sem("zeroed"), 1)

            pool.wait_ge(sem("kv_stored"), 64)
            zero(0)
            pool.wait_ge(sem("h_ready"), 2)
            pool.dma_start(hist, I["convT"]).then_inc(sem("hist_in"), 16)
            pool.dma_start(lru0, I["lruT"]).then_inc(sem("hist_in"), 16)
            pool.wait_ge(sem("ends_ready"), 1)
            pool.dma_start(O["lruT"], ends).then_inc(sem("ends_stored"), 16)
            pool.dma_start(O["convT"], cst).then_inc(sem("ends_stored"), 16)
            zero(1)
            pool.wait_ge(sem("hgrn_stored"), 16)
            pool.wait_ge(sem("ends_stored"), 32)

        @block.scalar
        def _(e):
            for name, dst in (("cT", cT[:, :, :]), ("cols", cols[:, :]), ("const", const[:, :]), ("xT", hT[:, :, :]),
                              ("rw", rw[:, :, :, :]), ("rb", rb[:, :, :])):
                e.dma_start(dst, I[name]).then_inc(sem(f"{name}_in"), 16)
            e.dma_start(S_END[:, 1:NSEQ, :, :], I["s0"]).then_inc(sem("s0_in"), 16)

            def norm(n):
                if n == 0:
                    e.wait_ge(sem("xT_in"), 16)
                    e.wait_ge(sem("const_in"), 16)
                else:
                    e.wait_ge(sem("h_ready"), n)
                for c in range(2):
                    e.activation(tmp[:, 4 * c:4 * c + 4, :], hT[:, 4 * c:4 * c + 4, :], ACT.Square)\
                        .then_inc(sem("sq_ready"), 1)
                e.wait_ge(sem("sumsq_ready"), n + 1)
                e.activation(stat[:, 0:2], ps[7][:, 0:2], ACT.Sqrt, bias=const[:, K_EPS:K_EPS + 1], scale=1.0 / D)\
                    .then_inc(sem("rms_ready"), 1)
                e.activation(stat[0:64, 2:3], ps[7][0:64, 2:3], ACT.Sqrt, bias=const[0:64, K_EPS:K_EPS + 1],
                             scale=1.0 / D).then_inc(sem("rms_ready"), 1)

            def router(l):
                for n, (dst, src) in enumerate(((rt[:, :, 4:8], rt[:, :, 0:4]), (rt[:, :, 41:42], rt[:, :, 40:41]))):
                    e.wait_ge(sem("rexp_in"), 2 * l + n + 1)
                    e.activation(dst, src, ACT.Exp).then_inc(sem("rexp_out"), 1)

            def dense(l):
                def expert(n, it=None):
                    for f in range(FT):
                        k = n * FT + f
                        base = 0 if it is None else it * (4 * FT)
                        e.wait_ge(sem(f"h1_ps{l}"), base + k + 1)
                        if it is not None or k >= 2:
                            e.wait_ge(sem(f"h13_used{l}"), base + k - 1)
                        e.activation(sig[:, f % 2, :], ps[2 * (f % 2)][:, 0:T], ACT.Sigmoid)\
                            .then_inc(sem(f"sg_ready{l}"), 1)
                for n in range(4):
                    expert(n)
                with e.Fori(1, 4) as it:
                    for n in range(4):
                        expert(n, it)

            def routed(l):
                def four(it=None):
                    def k(x, per):
                        return x if it is None else it * per + x
                    for d in range(DT):
                        e.wait_ge(sem(f"xe_ps{l}"), k(d + 1, DT))
                        e.copy(xe[:, d, :, :], ps[5 + d % 2][:, 0:4 * WIN].rearrange("p (e n) -> p e n", e=4))\
                            .then_inc(sem(f"xe_ev{l}"), 1)
                    for n in range(4):
                        e.wait_ge(sem(f"h1_ps{l}"), k(n + 1, 4))
                        if it is not None or n >= 2:
                            e.wait_ge(sem(f"act_in{l}"), k(n - 1, 4))
                        e.activation(sg[:, n % 2, :, :], ps[2 + n % 2][:, 0:FT * WIN].rearrange("p (f n) -> p f n", f=FT),
                                     ACT.Sigmoid).then_inc(sem(f"sg_ready{l}"), 1)
                        if n >= 2:
                            e.wait_ge(sem(f"ye_ps{l}"), k(n - 1, 2))
                            e.copy(ye[:, 1, :], ps[6][:, :]).then_inc(sem(f"ye_eva{l}"), 1)
                four()
                with e.Fori(1, 4) as it:
                    four(it)

            def experts(l):
                for n in range(6):
                    t, d0 = n // 2, 512 * (n % 2)
                    e.wait_ge(sem("utok_ps"), 6 * l + n + 1)
                    e.copy(utok[0:TROWS[t], t, d0:d0 + 512], ps[n % 4][0:TROWS[t], :]).then_inc(sem("utok_ev"), 1)
                router(l)
                e.wait_ge(sem("over_ready"), l + 1)
                over = e.value_load(over_i[0:1, 0:1], min_val=0, max_val=T)
                with e.If(over > 0):
                    dense(l)
                with e.Else():
                    routed(l)

            def ada_row(j, trips=None):
                k = 0 if trips is None else trips * RING
                e.wait_ge(sem("ada_ps"), k + j + 1)
                if trips is not None or j >= 2:
                    e.wait_ge(sem("ada_turned"), k + j - 1)
                e.copy(mrow[:, j % 2, :], ps[j % 2 if j < ADA_PIECES else 4][0:NSEQ, :]).then_inc(sem("ada_row"), 1)

            for j in range(RING):
                ada_row(j)
            with e.Fori(1, ADA_PIECES // RING) as it:
                for j in range(RING):
                    ada_row(j, it)
            e.wait_ge(sem("ada_turned"), ADA_PIECES)
            norm(0)
            e.wait_ge(sem("lb_in"), 1)
            e.activation(stat[:, 8:12], stat[:, 12:16], ACT.Sigmoid).then_inc(sem("lb_ready"), 1)
            for dst, src in ((xlag, 0), (tlag, 1), (wlag[0], 3)):
                e.wait_ge(sem("prj_ev"), 4 * (src + 1))
                e.activation(dst, prj[:, 4 * src:4 * src + 4, :], ACT.Sigmoid).then_inc(sem("hsig_ready"), 1)
            for j in range(ADA_PIECES, 2 * ADA_PIECES):
                ada_row(j)
            e.wait_ge(sem("inter_ev"), NCHUNK // 4)
            e.activation(tlag, oB, ACT.Square).then_inc(sem("osq_ready"), 1)
            e.wait_ge(sem("osum_ready"), 1)
            e.activation(stat[:, 16:24], ps[7][:, 0:8], ACT.Sqrt, bias=const[:, K_EPS:K_EPS + 1], scale=1.0 / P)\
                .then_inc(sem("orms_ready"), 1)
            e.activation(stat[0:64, 24:28], ps[7][0:64, 8:12], ACT.Sqrt, bias=const[0:64, K_EPS:K_EPS + 1],
                         scale=1.0 / P).then_inc(sem("orms_ready"), 1)
            for h in range(HEADS):
                e.wait_ge(sem("pmax_ready"), h + 1)
                for q, (lo, hi) in enumerate(((0, 128), (128, 384))):
                    e.activation(sc[:, h % 2, lo:hi], sc[:, h % 2, lo:hi], ACT.Exp, bias=sm[:, h % 2, q:q + 1],
                                 accum_out=sm[:, h % 2, 4 + q:5 + q]).then_inc(sem("pexp_ready"), 1)
            for s in range(4):
                e.wait_ge(sem("smax_ready"), s + 1)
                e.activation(sc[:, s % 2, 0:320], sc[:, s % 2, 0:320], ACT.Exp, bias=sm[:, s % 2, 0:1],
                             accum_out=sm[:, s % 2, 4:5]).then_inc(sem("sexp_ready"), 1)
            norm(1)
            experts(0)
            norm(2)
            e.wait_ge(sem("lam_in"), 1)
            e.activation(lsp[:, 1, :], lsp[:, 0, :], ACT.Exp, scale=-1.0).then_inc(sem("lam_out"), 1)
            for m in range(16):
                e.wait_ge(sem("lru_ready"), m + 1)
                dst, b = ((rT, C_BA), (iT, C_BX))[m // 8]
                e.activation(dst[:, m % 8, :], ps[4 + m % 4][:, 0:T], ACT.Sigmoid,
                             bias=cols[:, b + m % 8:b + m % 8 + 1]).then_inc(sem("lru_ev"), 1)
                if m == 7:
                    e.wait_ge(sem("gelu_in"), 1)
                    e.activation(t1, t1, ACT.Tanh).then_inc(sem("gelu_out"), 1)
            e.wait_ge(sem("loga_ready"), 1)
            e.activation(aT, rT, ACT.Exp).then_inc(sem("a_ready"), 1)
            e.activation(t1, rT, ACT.Tanh, scale=-1.0).then_inc(sem("a_ready"), 1)
            e.wait_ge(sem("om_ready"), 1)
            e.activation(t1, t1, ACT.Sqrt).then_inc(sem("root_ready"), 1)
            norm(3)
            experts(1)
            norm(4)
            e.wait_ge(sem("y_ready"), 1)
            e.dma_start(O["yT"], uT[:, :, :]).then_inc(sem("y_stored"), 16)
            e.wait_ge(sem("y_stored"), 16)

        @block.tensor
        def _(pe):
            mm = pe.matmul

            def piece(n, rounds=None):
                v = 16 * (n // RING + 1)
                pe.wait_ge(sem(f"piece_in{n % RING}"), v if rounds is None else rounds * 16 + v)

            gone = []

            def used(n):
                gone.append(n % RING)

            def group(out, pairs, first=True, final=True):
                for i, (a, b) in enumerate(pairs):
                    last = mm(out, a, b, start=(first and i == 0), stop=(final and i == len(pairs) - 1))
                    if gone and i < len(pairs) - 1:
                        last.then_inc(sem(f"piece_used{gone.pop(0)}"), 1)
                return last

            def norm(n):
                for c in range(2):
                    pe.wait_ge(sem("sq_ready"), 2 * n + c + 1)
                for t, rows in enumerate(TROWS):
                    last = group(ps[7][0:rows, t:t + 1],
                                 [(tmp[:, k, P * t:P * t + rows], ones[:, 0:1]) for k in range(DT)])
                last.then_inc(sem("sumsq_ready"), 1)
                pe.wait_ge(sem("rdiag_ready"), n + 1)
                for t, rows in enumerate(TROWS):
                    last = mm(ps[6][:, P * t:P * t + rows], ones[0:rows, :], diag[0:rows, t, 0:rows],
                              start=True, stop=True)
                last.then_inc(sem("rstd_ready"), 1)

            def project(at, src, name, n0=0, src_tiles=DT):
                piece(at)
                for m in range(4):
                    n = n0 + m
                    if n >= 4:
                        pe.wait_ge(sem(f"{name}_ev"), n - 3)
                    last = group(ps[n % 4][:, 0:T],
                                 [(w8[at % RING][:, k, P * m:P * m + P], src[:, k, :]) for k in range(DT)])
                    last.then_inc(sem(f"{name}_ps"), 1)
                used(at)

            pe.wait_ge(sem("cT_in"), 16)
            def ada_product(j, at, trips=None):
                k = 0 if trips is None else trips * RING
                bank = ps[j % 2 if j < ADA_PIECES else 4]
                piece(at, trips)
                if j >= ADA_PIECES:
                    pe.wait_ge(sem("ada_row"), j)
                elif trips is not None or j >= 2:
                    pe.wait_ge(sem("ada_row"), k + j - 1)
                group(bank[0:NSEQ, :], [(cT[:, kk, :], w8[at % RING][:, kk, :]) for kk in range(DT)])\
                    .then_inc(sem("ada_ps"), 1)
                used(at)

            def ada_turn(j, trips=None):
                k = 0 if trips is None else trips * RING
                pe.wait_ge(sem("ada_row"), k + j + 1)
                if trips is not None or j >= 1:
                    pe.wait_ge(sem("ada_ev"), k + j)
                bank = ps[2 if j < ADA_PIECES else 5]
                for m in range(4):
                    last = mm(bank[:, NSEQ * m:NSEQ * m + NSEQ], mrow[:, j % 2, P * m:P * m + P],
                              ident[0:NSEQ, 0:NSEQ], start=True, stop=True)
                last.then_inc(sem("ada_turned"), 1)

            pe.wait_ge(sem("const_in"), 16)
            for j in range(RING):
                ada_product(j, j)
                if j >= 1:
                    ada_turn(j - 1)
            with pe.Fori(1, ADA_PIECES // RING) as it:
                for j in range(RING):
                    ada_product(j, j, it)
                    ada_turn(j - 1, it)
            ada_turn(ADA_PIECES - 1)
            pe.wait_ge(sem("ones_ready"), 1)
            pe.wait_ge(sem("const_in"), 16)
            norm(0)
            pe.wait_ge(sem("u_ready"), 1)
            for i in range(4):
                project(AT_EVEN + i, uT, "prj", 4 * i)
            for d in range(CH):
                X = (xlag, xlag2)[d % 2]
                pe.wait_ge(sem("xlag_ready"), d + 1)
                if d >= 2:
                    pe.wait_ge(sem("lag_ev"), d - 1)
                for h in range(HG):
                    x = X[:, h, :].rearrange("p (c t) -> p c t", t=CH)[:, :, d:CH]
                    o = ps[4 * (d % 2) + h][:, 0:NCHUNK * (CH - d)].rearrange("p (c t) -> p c t", t=CH - d)
                    last = mm(o, ones[:, :], x, start=True, stop=True)
                last.then_inc(sem("lag_ps"), 1)

            def turn(t):
                rows = TROWS[t]
                if t == 0:
                    pe.wait_ge(sem("ktil_ready"), 1)
                for n, src in ((0, suf), (1, prj[:, 8:12, :])):
                    if 2 * t + n >= 1:
                        pe.wait_ge(sem("turn_ev"), 2 * t + n)
                    for h in range(HG):
                        last = pe.transpose(ps[7][0:rows, P * h:P * h + P], src[:, h, P * t:P * t + rows], ident)
                    last.then_inc(sem("turn_ps"), 1)

            def updates(G):
                t, p = G // 4, 32 * (G % 4)
                if G % 4 == 0:
                    pe.wait_ge(sem("turn_ev"), 2 * t + 2)
                for half in range(2):
                    u = 2 * G + half
                    if u >= 2:
                        pe.wait_ge(sem("chain"), u - 1)
                    for h in range(HG):
                        o = ps[2 * (u % 2) + h // 2][:, 256 * (h % 2):256 * (h % 2) + 256]\
                            .rearrange("p (c n) -> p c n", c=2)
                        last = mm(o, ktok[p:p + 32, t % 2, P * h:P * h + P],
                                  vexp[p:p + 32, t % 2, 2 * half:2 * half + 2, P * h:P * h + P],
                                  start=True, stop=True, skip_group_check=True)
                    last.then_inc(sem("upd_ps"), 1)

            def outputs(G):
                if G < 8:
                    pe.wait_ge(sem("chain"), 2 * G + 2)
                if G >= 1:
                    pe.wait_ge(sem("inter_ev"), G)
                for c in range(4):
                    j = 4 * G + c
                    for h in range(HG):
                        S = S_ST[:, j % 8, h, :] if G < 8 else S_END[:, j - 31, h, :]
                        last = mm(ps[6][:, 32 * h + 8 * c:32 * h + 8 * c + 8], S, prj[:, h, 8 * j:8 * j + 8],
                                  start=True, stop=True)
                last.then_inc(sem("inter_ps"), 1)

            pe.wait_ge(sem("lag_ev"), CH)
            turn(0)
            updates(0)
            beside = ADA_PIECES
            for G in range(NCHUNK // 4):
                if G % 4 == 1 and G // 4 + 1 < TT:
                    turn(G // 4 + 1)
                if G < 8:
                    updates(G + 1)
                for _ in range(ADA_BESIDE[G]):
                    ada_product(beside, AT_ADA1 + beside - ADA_PIECES)
                    if beside > ADA_PIECES:
                        ada_turn(beside - 1)
                    beside += 1
                outputs(G)
                if G == 8:
                    updates(9)
            ada_turn(beside - 1)
            pe.wait_ge(sem("osq_ready"), 1)
            for t, rows in enumerate(TROWS):
                for h in range(HG):
                    last = mm(ps[7][0:rows, 4 * t + h:4 * t + h + 1], tlag[:, h, P * t:P * t + rows], ones[:, 0:1],
                              start=True, stop=True)
            last.then_inc(sem("osum_ready"), 1)
            pe.wait_ge(sem("odiag_ready"), 1)
            for h in range(HG):
                for t, rows in enumerate(TROWS):
                    last = mm(ps[h][:, P * t:P * t + rows], ones[0:rows, :], odiag[0:rows, t, h, 0:rows],
                              start=True, stop=True)
            last.then_inc(sem("orstd_ready"), 1)

            pe.wait_ge(sem("hgrn_done"), 1)
            n = 0
            for i in range(3):
                piece(AT_QKV + i)
                for t, rows in enumerate(TROWS):
                    if n >= 6:
                        pe.wait_ge(sem("qkv_ev"), n - 5)
                    last = group(ps[n % 6][0:rows, :], [(uT[:, k, P * t:P * t + rows], w8[(AT_QKV + i) % RING][:, k, :])
                                                        for k in range(DT)])
                    last.then_inc(sem("qkv_ps"), 1)
                    n += 1
                used(AT_QKV + i)
            for src in (qtok, ktk):
                for t, rows in enumerate(TROWS):
                    pe.wait_ge(sem("qkv_ev"), max(n - 5, 6))
                    for p in range(PAIRS):
                        last = pe.transpose(ps[n % 6][:, P * p:P * p + rows], src[0:rows, t, P * p:P * p + P],
                                            ident[0:rows, 0:rows])
                    last.then_inc(sem("qkv_ps"), 1)
                    n += 1
            qT, kTn = qkT[:, 0, :, :], qkT[:, 1, :, :]
            pe.wait_ge(sem("qkv_ev"), 15)

            def prompt_scores(h):
                p, e = h // 2, 64 * (h % 2)
                if h >= 2:
                    pe.wait_ge(sem("pmask_done"), h - 1)
                o = ps[h % 2]
                mm(o[:, 0:128], qT[e:e + 64, p, 0:128], kTn[e:e + 64, p, 0:128], start=True, stop=True)
                mm(o[:, 128:384], qT[e:e + 64, p, 128:256], kTn[e:e + 64, p, 0:256], start=True, stop=True)\
                    .then_inc(sem("pscore_ps"), 1)

            def prompt_values(h):
                p, e = h // 2, 64 * (h % 2)
                pe.wait_ge(sem("p_ready"), h + 1)
                if h >= 2:
                    pe.wait_ge(sem("pT_ready"), h - 1)
                for j in range(3):
                    last = pe.transpose(ps[2 + h % 2][:, P * j:P * j + P], sc[:, h % 2, P * j:P * j + P], ident)
                last.then_inc(sem("pT_ps"), 1)
                pe.wait_ge(sem("pT_ready"), h + 1)
                if h >= 4 and h % 2 == 0:
                    pe.wait_ge(sem("ppv_ev"), p - 1)
                o = ps[4 + p % 2]
                mm(o[e:e + 64, 0:128], vtok[:, 0, 64 * h:64 * h + 64], pT[:, h % 2, 0:128], start=True, stop=True)
                group(o[e:e + 64, 128:256], [(vtok[:, j, 64 * h:64 * h + 64], pT[:, h % 2, P + P * j:2 * P + P * j])
                                             for j in range(2)]).then_inc(sem("ppv_ps"), 1)

            for h in range(HEADS + 1):
                if h < HEADS:
                    prompt_scores(h)
                if h >= 1:
                    prompt_values(h - 1)

            def sample_scores(s):
                if s == 0:
                    pe.wait_ge(sem("qx_ready"), 1)
                    pe.wait_ge(sem("pmask_done"), HEADS)
                if s >= 2:
                    pe.wait_ge(sem("smask_done"), s - 1)
                for e in range(2):
                    b = 2 * s + e
                    pe.wait_ge(sem(f"past_in{b % 4}"), 64 * (b // 4 + 1))
                    o = ps[s % 2][64 * e:64 * e + 64, :]
                    group(o[:, 0:256].rearrange("p (g n) -> p g n", g=2),
                          [(QX[:, p, 2 * s + e, :], KV[b % 4][:, 0, :, P * p:P * p + P]) for p in range(PAIRS)])
                    last = group(o[:, 256:320], [(QX[:, p, 2 * s + e, :], kTn[:, p, 256:320]) for p in range(PAIRS)])
                last.then_inc(sem("sscore_ps"), 1)

            def sample_values(s):
                pe.wait_ge(sem("s_ready"), s + 1)
                if s == 0:
                    pe.wait_ge(sem("pT_ready"), HEADS)
                    pe.wait_ge(sem("ppv_ev"), PAIRS)
                if s >= 2:
                    pe.wait_ge(sem("sT_ready"), s - 1)
                for j in range(2):
                    pe.transpose(ps[2 + s % 2][:, P * j:P * j + P], sc[:, s % 2, P * j:P * j + P], ident)
                pe.transpose(ps[2 + s % 2][0:64, 256:384], sc[:, s % 2, 256:320], ident).then_inc(sem("sT_ps"), 1)
                pe.wait_ge(sem("sT_ready"), s + 1)
                if s >= 2:
                    pe.wait_ge(sem("spv_ev"), s - 1)
                for e in range(2):
                    for p in range(PAIRS):
                        c = 64 * e + 16 * p
                        last = group(ps[4 + s % 2][:, c:c + 16],
                                     [(KV[(2 * s + e) % 4][:, 1, g, P * p:P * p + P], pT[:, s % 2, P * g + c:P * g + c + 16])
                                      for g in range(2)]
                                     + [(vtok[0:64, 2, P * p:P * p + P], pT[0:64, s % 2, 256 + c:256 + c + 16])])
                    last.then_inc(sem("spv_used"), 1)

            for s in range(4):
                sample_scores(s)
                sample_values(s)

            def project_out(at, src, name):
                for i in range(2):
                    project(at + i, src, name, 4 * i)

            pe.wait_ge(sem("spv_ev"), 4)
            project_out(AT_EVEN_OUT, mixT, "res0")

            def router(l):
                pe.wait_ge(sem("u_ready"), 2 * l + 2)
                if l == 0:
                    pe.wait_ge(sem("rw_in"), 16)
                    pe.wait_ge(sem("rb_in"), 16)
                for t, rows in enumerate(TROWS):
                    last = group(ps[5][0:rows, 20 * t:20 * t + 20],
                                 [(uT[:, k, P * t:P * t + rows], rw[:, l, k, :]) for k in range(DT)]
                                 + [(ones[0:1, 0:rows], rb[0:1, l, :])])
                last.then_inc(sem("logits_ps"), 1)

            def dense(l):
                def expert(n, it=None):
                    at1, at3, at2 = (AT_MOE[l] + w[n] for w in (W1, W3, W2))
                    r3 = None if it is None else it * 3

                    def k(v, per):
                        return v if it is None else it * (4 * per) + v
                    pe.wait_ge(sem(f"cdiag_ready{l}"), k(n + 1, 1))
                    for t, rows in enumerate(TROWS):
                        last = mm(ps[7][:, P * t:P * t + rows], ones[0:rows, :], cdiag[0:rows, t, 0:rows],
                                  start=True, stop=True)
                    last.then_inc(sem(f"cb_ps{l}"), 1)
                    piece(at1, r3)
                    piece(at3, r3)
                    for f in range(FT):
                        g = FT * n + f
                        if it is not None or g >= 2:
                            pe.wait_ge(sem(f"h13_used{l}"), k(g - 1, FT))
                        for i, at in enumerate((at1, at3)):
                            w = w8[at % RING]
                            last = group(ps[2 * (f % 2) + i][:, 0:T],
                                         [(w[:, kk, P * f:P * f + P], uT[:, kk, :]) for kk in range(DT)])
                            if f == FT - 1:
                                used(at)
                        last.then_inc(sem(f"h1_ps{l}"), 1)
                    piece(at2, r3)
                    pe.wait_ge(sem(f"act_ready{l}"), k(FT * (n + 1), FT))
                    for m in range(DT):
                        g = DT * n + m
                        if it is not None or g >= 3:
                            pe.wait_ge(sem(f"out_ev{l}"), k(g - 2, DT))
                        last = group(ps[4 + m % 3][:, 0:T],
                                     [(w4[at2 % RING][:, f, P * m:P * m + P], act[:, n % 2, f, :]) for f in range(FT)])
                        last.then_inc(sem(f"out_ps{l}"), 1)
                    used(at2)
                for n in range(4):
                    expert(n)
                with pe.Fori(1, 4) as it:
                    for n in range(4):
                        expert(n, it)
                group(ps[7][:, 0:1], [(ones[:, :], ones[:, 0:1])] * 2)

            def slots(l):
                for n in range(6):
                    t, d0 = n // 2, 4 * (n % 2)
                    rows = TROWS[t]
                    if n >= 4:
                        pe.wait_ge(sem("utok_ev"), 6 * l + n - 3)
                    for d in range(4):
                        last = pe.transpose(ps[n % 4][0:rows, P * d:P * d + P], uT[:, d0 + d, P * t:P * t + rows], ident)
                    last.then_inc(sem("utok_ps"), 1)
                pe.wait_ge(sem("sel_ready"), l + 1)
                tri = const[:, K_TRI:K_TRI + P]
                for t, rows in enumerate(TROWS):
                    group(ps[6][0:rows, NE * t:NE * t + NE],
                          [(ones[:, 0:rows], sel[:, i, :]) for i in range(t)] + [(tri[0:rows, 0:rows], sel[0:rows, t, :])])
                group(ps[6][:, 64:64 + NE], [(ones[0:r, :], sel[0:r, t, :]) for t, r in enumerate(TROWS)])\
                    .then_inc(sem("pos_ps"), 1)

            def routed(l):
                def four(it=None):
                    def k(x, per):
                        return x if it is None else it * per + x
                    later = it is not None
                    r3 = it * 3 if later else None
                    at1, at3, at2 = ([AT_MOE[l] + x for x in w] for w in (W1, W3, W2))
                    pe.wait_ge(sem(f"pick_ready{l}"), k(1, 1))
                    if not later:
                        pe.wait_ge(sem("utok_ev"), 6 * l + 6)
                    for d in range(DT):
                        if later or d >= 2:
                            pe.wait_ge(sem(f"xe_ev{l}"), k(d - 1, DT))
                        last = group(ps[5 + d % 2][:, 0:4 * WIN].rearrange("p (e n) -> p e n", e=4),
                                     [(utok[0:r, t, P * d:P * d + P], pick[0:r, t, :, :]) for t, r in enumerate(TROWS)])
                        last.then_inc(sem(f"xe_ps{l}"), 1)
                    pe.wait_ge(sem(f"xe_ev{l}"), k(DT, DT))

                    def hidden(e, at, bank, name):
                        piece(at, r3)
                        if name == "h1" and (later or e >= 2):
                            pe.wait_ge(sem(f"act_in{l}"), k(e - 1, 4))
                        if name == "h3" and (later or e >= 1):
                            pe.wait_ge(sem(f"act_in{l}"), k(e, 4))
                        for f in range(FT):
                            last = group(ps[bank][:, WIN * f:WIN * f + WIN],
                                         [(w8[at % RING][:, kk, P * f:P * f + P], xe[:, kk, e, :]) for kk in range(DT)])
                        last.then_inc(sem(f"{name}_ps{l}"), 1)
                        used(at)

                    def outputs_of(e):
                        at, pair = at2[e], e // 2
                        piece(at, r3)
                        if e % 2 == 0 and (later or pair >= 1):
                            pe.wait_ge(sem(f"ye_evv{l}"), k(pair, 2))
                            pe.wait_ge(sem(f"ye_eva{l}"), k(pair, 2))
                        pe.wait_ge(sem(f"act_in{l}"), k(e + 1, 4))
                        for half in range(2):
                            last = group(ps[5 + half], [(acts[:, e, f, :], w4[at % RING][:, f, 512 * half:512 * half + 512])
                                                        for f in range(FT)], first=(e % 2 == 0), final=(e % 2 == 1))
                        if e % 2:
                            last.then_inc(sem(f"ye_ps{l}"), 1)
                        used(at)

                    def scatter(pair):
                        pe.wait_ge(sem(f"spread_ready{l}"), k(pair + 1, 2))
                        if later or pair >= 1:
                            pe.wait_ge(sem(f"out_ev{l}"), k(8 * pair - 2, 16))
                        for t, r in enumerate(TROWS):
                            last = group(ps[1][:, P * t:P * t + r], [(spread[0:r, i, t, :], ident[0:r, 0:r]) for i in range(2)])
                        last.then_inc(sem(f"back_ps{l}"), 1)
                        pe.wait_ge(sem(f"ye_evv{l}"), k(pair + 1, 2))
                        pe.wait_ge(sem(f"ye_eva{l}"), k(pair + 1, 2))
                        pe.wait_ge(sem(f"back_ev{l}"), k(pair + 1, 2))
                        for d in range(DT):
                            if d >= 3:
                                pe.wait_ge(sem(f"out_ev{l}"), k(8 * pair + d - 2, 16))
                            elif d < 2 and (later or pair >= 1):
                                pe.wait_ge(sem(f"out_ev{l}"), k(8 * pair + d - 1, 16))
                            mm(ps[(7, 0, 1)[d % 3]][:, 0:T], ye[:, d // 4, P * (d % 4):P * (d % 4) + P], back,
                               start=True, stop=True).then_inc(sem(f"out_ps{l}"), 1)

                    hidden(0, at1[0], 2, "h1")
                    hidden(0, at3[0], 4, "h3")
                    hidden(1, at1[1], 3, "h1")
                    outputs_of(0)
                    hidden(1, at3[1], 4, "h3")
                    hidden(2, at1[2], 2, "h1")
                    outputs_of(1)
                    hidden(2, at3[2], 4, "h3")
                    scatter(0)
                    hidden(3, at1[3], 3, "h1")
                    outputs_of(2)
                    hidden(3, at3[3], 4, "h3")
                    outputs_of(3)
                    scatter(1)
                four()
                with pe.Fori(1, 4) as it:
                    four(it)

            def experts(l):
                slots(l)
                pe.wait_ge(sem("over_ready"), l + 1)
                over = pe.value_load(over_i[0:1, 0:1], min_val=0, max_val=T)
                before = list(gone)
                with pe.If(over > 0):
                    dense(l)
                after = list(gone)
                gone[:] = before
                with pe.Else():
                    routed(l)
                assert gone == after

            norm(1)
            router(0)
            experts(0)
            norm(2)
            pe.wait_ge(sem("u_ready"), 3)
            for i in range(4):
                project(AT_ODD + i, uT, "odd", 4 * i)
            pe.wait_ge(sem("conv_ready"), CONV)
            piece(AT_LRU)
            wl = ring[AT_LRU % RING][:, :].rearrange("p (g h k n) -> p g h k n", g=2, h=4, k=2)
            for m in range(16):
                g, h, j = m // 8, m % 8 // 2, m % 2
                if m >= 4:
                    pe.wait_ge(sem("lru_ev"), m - 3)
                last = group(ps[4 + m % 4][:, 0:T], [(wl[:, g, h, k, P * j:P * j + P], xc[:, 2 * h + k, :]) for k in range(2)])
                last.then_inc(sem("lru_ready"), 1)
            used(AT_LRU)
            pe.wait_ge(sem("odd_mix_ready"), 1)
            project_out(AT_ODD_OUT, xc, "res1")
            norm(3)
            router(1)
            experts(1)
            norm(4)
            assert not gone

        @block.vector
        def _(v):
            step = Chain(v, sem("v_step"))
            tt, ts, stt, cp = v.tensor_tensor, v.tensor_scalar, v.scalar_tensor_tensor, v.tensor_copy
            MUL, ADD, SUB, MAX, MIN, EQ, GE = ALU.mult, ALU.add, ALU.subtract, ALU.max, ALU.min, ALU.is_equal, ALU.is_ge

            def over(ap, n, axis=2):
                s = list(ap.shape)
                return ap.unsqueeze(axis).broadcast_to(s[:axis] + [n] + s[axis:])

            def bt(x):
                return x.rearrange("p (b t) -> p b t", t=S_LEN)

            def bt3(x):
                return x.rearrange("p m (b t) -> p m b t", t=S_LEN)

            def norm(n):
                v.wait_ge(sem("rms_ready"), 2 * n + 2)
                step(v.reciprocal(stat[:, 4:6], stat[:, 0:2]))
                step(v.reciprocal(stat[0:64, 6:7], stat[0:64, 2:3]))
                for t, rows in enumerate(TROWS):
                    last = ts(diag[0:rows, t, :], ident[0:rows, :], stat[0:rows, 4 + t:5 + t], None, MUL)
                last.then_inc(sem("rdiag_ready"), 1)
                v.wait_ge(sem("rstd_ready"), n + 1)
                step(tt(tmp[:, :, :], hT[:, :, :], over(ps[6][:, 0:T], DT, 1), MUL))
                if n == 4:
                    for m in range(DT):
                        last = ts(uT[:, m, :], tmp[:, m, :], cols[:, C_NFIN + m:C_NFIN + m + 1], None, MUL)
                    last.then_inc(sem("y_ready"), 1)
                    return
                for m in range(DT):
                    ts(uT[:, m, 0:NP_TOK], tmp[:, m, 0:NP_TOK], gain[:, n, m, 0:1], shift(n)[:, m, 0:1], MUL, ADD)
                step(tt(bt3(uT[:, :, NP_TOK:T]), bt3(tmp[:, :, NP_TOK:T]), over(gain[:, n, :, 1:NSEQ], S_LEN, 3), MUL))
                tt(bt3(uT[:, :, NP_TOK:T]), bt3(uT[:, :, NP_TOK:T]), over(shift(n)[:, :, 1:NSEQ], S_LEN, 3), ADD)\
                    .then_inc(sem("u_ready"), 1)

            def residual(n, name):
                for m in range(DT):
                    v.wait_ge(sem(f"{name}_ps"), m + 1)
                    src = ps[m % 4]
                    step(tt(bt(sadd[:, m % 2, :]), bt(src[:, NP_TOK:T]), over(gate(n)[:, m, 1:NSEQ], S_LEN), MUL))
                    stt(hT[:, m, 0:NP_TOK], src[:, 0:NP_TOK], gate(n)[:, m, 0:1], hT[:, m, 0:NP_TOK], MUL, ADD)\
                        .then_inc(sem(f"{name}_ev"), 1)
                    last = tt(hT[:, m, NP_TOK:T], hT[:, m, NP_TOK:T], sadd[:, m % 2, :], ADD)
                last.then_inc(sem("h_ready"), 1)

            def top1(src, m, eq, c, oh):
                step(v.tensor_reduce(rt[:, :, m:m + 1], src, AX, MAX))
                step(tt(rt[:, :, eq:eq + 4], src, rt[:, :, m:m + 1].broadcast_to([P, TT, 4]), GE))
                step(tt(rt[:, :, eq:eq + 4], rt[:, :, eq:eq + 4], over(const[:, K_RANK:K_RANK + 4], TT, 1), MUL))
                step(v.tensor_reduce(rt[:, :, c:c + 1], rt[:, :, eq:eq + 4], AX, MAX))
                step(tt(rt[:, :, oh:oh + 4], rt[:, :, eq:eq + 4], rt[:, :, c:c + 1].broadcast_to([P, TT, 4]), EQ))

            def router(l):
                if l == 0:
                    v.wait_ge(sem("kv_stored"), 64)
                step(v.memset(lg, 0.0))
                v.memset(comb[:, :, NE:NE + 4], 0.0)
                v.wait_ge(sem("logits_ps"), l + 1)
                cp(lg[:, 0:2, :], ps[5][:, 0:40].rearrange("p (t n) -> p t n", t=2))
                step(cp(lg[0:64, 2, :], ps[5][0:64, 40:60]))
                top1(lg[:, :, 0:4], 8, 12, 16, 20)
                tt(rt[:, :, 0:4], lg[:, :, 0:4], rt[:, :, 8:9].broadcast_to([P, TT, 4]), SUB).then_inc(sem("rexp_in"), 1)
                for g in range(GROUPS):
                    last = tt(rt[:, :, 24 + 4 * g:28 + 4 * g], lg[:, :, 4 + 4 * g:8 + 4 * g],
                              rt[:, :, 20 + g:21 + g].broadcast_to([P, TT, 4]), MUL)
                step(last)
                step(tt(rt[:, :, 24:32], rt[:, :, 24:32], rt[:, :, 32:40], ADD))
                step(tt(rt[:, :, 44:48], rt[:, :, 24:28], rt[:, :, 28:32], ADD))
                top1(rt[:, :, 44:48], 48, 12, 16, 52)
                step(stt(rt[:, :, 56:60], rt[:, :, 52:56], FAR, rt[:, :, 44:48], MUL, ADD))
                top1(rt[:, :, 56:60], 60, 12, 16, 64)
                tt(rt[:, :, 40:41], rt[:, :, 60:61], rt[:, :, 48:49], SUB).then_inc(sem("rexp_in"), 1)
                v.wait_ge(sem("rexp_out"), 2 * l + 2)
                step(v.tensor_reduce(rt[:, :, 9:10], rt[:, :, 4:8], AX, ADD))
                step(ts(rt[:, :, 10:11], rt[:, :, 41:42], 1.0, None, ADD))
                step(tt(rt[:, :, 10:11], rt[:, :, 10:11], rt[:, :, 9:10], MUL))
                step(v.reciprocal(rt[:, :, 68:69], rt[:, :, 10:11]))
                step(tt(rt[:, :, 69:70], rt[:, :, 68:69], rt[:, :, 41:42], MUL))
                tt(rt[:, :, 52:56], rt[:, :, 52:56], rt[:, :, 68:69].broadcast_to([P, TT, 4]), MUL)
                step(tt(rt[:, :, 64:68], rt[:, :, 64:68], rt[:, :, 69:70].broadcast_to([P, TT, 4]), MUL))
                step(tt(rt[:, :, 72:76], rt[:, :, 52:56], rt[:, :, 64:68], ADD))
                for g in range(GROUPS):
                    last = tt(comb[:, :, 4 * g:4 * g + 4], rt[:, :, 72:76],
                              rt[:, :, 20 + g:21 + g].broadcast_to([P, TT, 4]), MUL)
                step(last)

            def slots(l):
                sgn, off = const[:, K_SGN:K_SGN + NE], const[:, K_OFF:K_OFF + NE]
                slots_ = slot[:, :, 0:NE]
                step(ts(sel, comb[:, :, 0:NE], 0.0, None, ALU.is_gt))
                v.memset(slot, 0.0).then_inc(sem("sel_ready"), 1)
                v.wait_ge(sem("sel_ready"), l + 1)
                v.wait_ge(sem("pos_ps"), l + 1)
                cp(slot[:, 0:2, 0:NE], ps[6][:, 0:2 * NE].rearrange("p (t n) -> p t n", t=2))
                step(cp(slot[0:64, 2, 0:NE], ps[6][0:64, 2 * NE:3 * NE]))
                v.tensor_reduce(fits[0:1, 0:1], ps[6][0:1, 64:64 + NE], AX, MAX)
                v.tensor_reduce(fits[0:1, 4:12], ps[6][0:1, 64:64 + NE].rearrange("p (a b) -> p a b", b=2), AX, ADD)
                step(tt(slots_, slots_, over(sgn, TT, 1), MUL))
                step(v.tensor_reduce(fits[0:1, 1:2], fits[0:1, 4:12], AX, MAX))
                ts(fits[0:1, 0:1], fits[0:1, 0:1], -float(WIN), None, ADD)
                ts(fits[0:1, 1:2], fits[0:1, 1:2], -float(SLOTS), None, ADD)
                step(tt(slots_, slots_, over(off, TT, 1), ADD))
                step(ts(fits[0:1, 2:3], fits[0:1, 0:1], fits[0:1, 1:2], None, MAX))
                step(tt(slots_, slots_, sel, MUL))
                ts(over_i[0:1, 0:1], fits[0:1, 2:3], 0.0, None, MAX).then_inc(sem("over_ready"), 1)
                step(ts(slots_, slots_, -NOWHERE, None, ADD))

            def routed(l):
                link = Chain(v, sem(f"expert_step{l}"))
                iota = const[:, K_IOTA:K_IOTA + SLOTS]

                def picks(after=None):
                    at = slice(0, 4) if after is None else bass.ds(after * 4 + 4, 4)
                    cp(now[:, 0, :, :], slot[:, :, at])
                    link(cp(now[:, 1, :, :], comb[:, :, at]))
                    for e in range(4):
                        w = iota[:, 0:WIN] if e % 2 == 0 else iota[:, SLOTS - WIN:SLOTS]
                        last = tt(pick[:, :, e, :], over(w, TT, 1), now[:, 0, :, e:e + 1].broadcast_to([P, TT, WIN]), EQ)
                    last.then_inc(sem(f"pick_ready{l}"), 1)

                def four(it=None):
                    def k(x, per):
                        return x if it is None else it * per + x
                    later = it is not None

                    def spread_pair(pair):
                        if later or pair >= 1:
                            v.wait_ge(sem(f"back_ps{l}"), k(pair, 2))
                        for i in range(2):
                            for t, r in enumerate(TROWS):
                                e = 2 * pair + i
                                last = ts(spread[0:r, i, t, :], iota[0:r, :], now[0:r, 0, t, e:e + 1],
                                          now[0:r, 1, t, e:e + 1], EQ, MUL)
                        last.then_inc(sem(f"spread_ready{l}"), 1)

                    def gated(e):
                        lo = 0 if e % 2 == 0 else SLOTS - WIN
                        a, s = acts[:, e, :, lo:lo + WIN], sg[:, e % 2, :, :]
                        h1, h3 = (ps[b][:, 0:FT * WIN].rearrange("p (f n) -> p f n", f=FT) for b in (2 + e % 2, 4))
                        v.wait_ge(sem(f"sg_ready{l}"), k(e + 1, 4))
                        link(tt(s, s, h1, MUL))
                        v.wait_ge(sem(f"h3_ps{l}"), k(e + 1, 4))
                        tt(a, s, h3, MUL).then_inc(sem(f"act_in{l}"), 1)

                    def half_out(pair):
                        v.wait_ge(sem(f"ye_ps{l}"), k(pair + 1, 2))
                        cp(ye[:, 0, :], ps[5][:, :]).then_inc(sem(f"ye_evv{l}"), 1)

                    def gather_out(pair):
                        v.wait_ge(sem(f"back_ps{l}"), k(pair + 1, 2))
                        cp(back, ps[1][:, 0:T]).then_inc(sem(f"back_ev{l}"), 1)

                    def add_out(pair):
                        for d in range(DT):
                            v.wait_ge(sem(f"out_ps{l}"), k(8 * pair + d + 1, 16))
                            tt(yacc[:, d, :], yacc[:, d, :], ps[(7, 0, 1)[d % 3]][:, 0:T], ADD).then_inc(sem(f"out_ev{l}"), 1)

                    spread_pair(0)
                    gated(0)
                    gated(1)
                    half_out(0)
                    gated(2)
                    gather_out(0)
                    add_out(0)
                    spread_pair(1)
                    gated(3)
                    picks(0 if it is None else it)
                    half_out(1)
                    gather_out(1)
                    add_out(1)
                    v.wait_ge(sem(f"out_ev{l}"), k(16, 16))
                picks()
                four()
                with v.Fori(1, 4) as it:
                    link.enter(it - 1, 5)
                    four(it)
                    link.leave(3)

            def experts(l):
                slots(l)
                v.wait_ge(sem("zeroed"), 2 * l + 2)
                v.wait_ge(sem("over_ready"), l + 1)
                full = v.value_load(over_i[0:1, 0:1], min_val=0, max_val=T)
                with v.If(full > 0):
                    dense(l)
                with v.Else():
                    routed(l)
                n = 2 * l + 1
                for m in range(DT):
                    stt(hT[:, m, 0:NP_TOK], yacc[:, m, 0:NP_TOK], gate(n)[:, m, 0:1], hT[:, m, 0:NP_TOK], MUL, ADD)
                step(tt(bt3(yacc[:, :, NP_TOK:T]), bt3(yacc[:, :, NP_TOK:T]), over(gate(n)[:, :, 1:NSEQ], S_LEN, 3), MUL))
                tt(hT[:, :, NP_TOK:T], hT[:, :, NP_TOK:T], yacc[:, :, NP_TOK:T], ADD).then_inc(sem("h_ready"), 1)

            def dense(l):
                step = Chain(v, sem(f"expert_step{l}"))

                def expert(n, it=None):
                    def k(x, per):
                        return x if it is None else it * (4 * per) + x
                    if it is not None or n >= 1:
                        v.wait_ge(sem(f"cb_ps{l}"), k(n, 1))
                    for t, rows in enumerate(TROWS):
                        c = comb[0:rows, t, n:n + 1] if it is None else comb[0:rows, t, bass.ds(it * 4 + n, 1)]
                        last = ts(cdiag[0:rows, t, :], ident[0:rows, :], c, None, MUL)
                    last.then_inc(sem(f"cdiag_ready{l}"), 1)
                    v.wait_ge(sem(f"cb_ps{l}"), k(n + 1, 1))
                    step(cp(cb[:, n % 2, :], ps[7][:, 0:T]))
                    for f in range(FT):
                        v.wait_ge(sem(f"sg_ready{l}"), k(FT * n + f + 1, FT))
                        s, h1, h3 = sig[:, f % 2, :], ps[2 * (f % 2)][:, 0:T], ps[2 * (f % 2) + 1][:, 0:T]
                        a = act[:, n % 2, f, :]
                        step(tt(a, s, h1, MUL))
                        tt(a, a, h3, MUL).then_inc(sem(f"h13_used{l}"), 1)
                        v.wait_ge(sem(f"h13_used{l}"), k(FT * n + f + 1, FT))
                        tt(a, a, cb[:, n % 2, :], MUL).then_inc(sem(f"act_ready{l}"), 1)
                    for m in range(DT):
                        v.wait_ge(sem(f"out_ps{l}"), k(DT * n + m + 1, DT))
                        tt(yacc[:, m, :], yacc[:, m, :], ps[4 + m % 3][:, 0:T], ADD).then_inc(sem(f"out_ev{l}"), 1)
                    v.wait_ge(sem(f"out_ev{l}"), k(DT * (n + 1), DT))
                for n in range(4):
                    expert(n)
                with v.Fori(1, 4) as it:
                    step.enter(it - 1, 4 * (1 + FT))
                    for n in range(4):
                        expert(n, it)
                    step.leave(3)

            v.wait_ge(sem("cols_in"), 16)
            v.wait_ge(sem("const_in"), 16)
            tt(stat[:, 12:16], cols[:, C_LB:C_LB + 4], cols[:, C_LB + 4:C_LB + 8], SUB).then_inc(sem("lb_in"), 1)
            flat_mods = mods[:, :, :, :].rearrange("p l m b -> p (l m) b")

            def ada(j, trips=None):
                at = 4 * j if trips is None else trips * (4 * RING) + 4 * j
                v.wait_ge(sem("ada_turned"), j + 1 if trips is None else trips * RING + (j + 1))
                tt(flat_mods[:, bass.ds(at, 4), :],
                   ps[2 if j < ADA_PIECES else 5][:, 0:4 * NSEQ].rearrange("p (m b) -> p m b", b=NSEQ),
                   over(cols[:, bass.ds(at + C_ADAB, 4)], NSEQ), ADD).then_inc(sem("ada_ev"), 1)

            def gains(l):
                v.wait_ge(sem("ada_ev"), ADA_PIECES * (l + 1))
                for w in range(2):
                    c = (C_NMIX, C_NFFN)[w] + 8 * l
                    last = stt(gain[:, 2 * l + w, :, :], mods[:, l, 24 * w + 8:24 * w + 16, :], 1.0,
                               over(cols[:, c:c + 8], NSEQ), ADD, MUL)
                step(last)

            for j in range(RING):
                ada(j)
            with v.Fori(1, ADA_PIECES // RING) as it:
                for j in range(RING):
                    ada(j, it)
            gains(0)
            norm(0)
            for n in range(16):
                v.wait_ge(sem("prj_ps"), n + 1)
                cp(prj[:, n, :], ps[n % 4][:, 0:T]).then_inc(sem("prj_ev"), 1)
            v.wait_ge(sem("lb_ready"), 1)
            v.wait_ge(sem("hsig_ready"), 3)
            v.wait_ge(sem("prj_ev"), 16)
            step(ts(stat[:, 28:32], stat[:, 8:12], -1.0, 1.0, MUL, ADD))
            tt(prj[:, 0:4, :], prj[:, 0:4, :], xlag, MUL)
            tt(prj[:, 12:16, :], prj[:, 12:16, :], wlag[0], MUL)
            for h in range(HG):
                last = ts(prj[:, 4 + h, :], tlag[:, h, :], stat[:, 28 + h:29 + h], stat[:, 8 + h:9 + h], MUL, ADD)
            step(last)
            q_, f_, v_ = prj[:, 0:4, :], prj[:, 4:8, :], prj[:, 8:12, :]

            def c8(x):
                return x.rearrange("p h (c t) -> p (h c) t", t=CH)

            def lag_out(d):
                v.wait_ge(sem("lag_ps"), d + 1)
                s = banks[:, 4 * (d % 2):4 * (d % 2) + 4, 0:NCHUNK * (CH - d)].rearrange("p h (c t) -> p h c t", t=CH - d)
                vals = v_.rearrange("p h (c t) -> p h c t", t=CH)[:, :, :, 0:CH - d]
                dst = (oB if d == 0 else tlag).rearrange("p h (c t) -> p h c t", t=CH)[:, :, :, d:CH]
                last = tt(dst, s, vals, MUL)
                last.then_inc(sem("lag_ev"), 1)
                v.wait_ge(sem("lag_ev"), d + 1)
                if d:
                    step(tt(c8(oB)[:, :, d:CH], c8(oB)[:, :, d:CH], c8(tlag)[:, :, d:CH], ADD))

            step(ts(kf, f_, -1.0, 1.0, MUL, ADD))
            for d in range(CH):
                X, W, W0 = (xlag, xlag2)[d % 2], wlag[d % 2], (wlag[(d + 1) % 2] if d > 1 else kf)
                if d >= 2:
                    v.wait_ge(sem("lag_ps"), d - 1)
                if d == 0:
                    tt(X, q_, kf, MUL).then_inc(sem("xlag_ready"), 1)
                else:
                    step(tt(c8(W)[:, :, d:CH], c8(f_)[:, :, d:CH], c8(W0)[:, :, d - 1:CH - 1], MUL))
                    tt(c8(X)[:, :, d:CH], c8(q_)[:, :, d:CH], c8(W)[:, :, d:CH], MUL).then_inc(sem("xlag_ready"), 1)
                if d >= 1:
                    lag_out(d - 1)
            lag_out(CH - 1)

            cp(c8(pre)[:, :, 0:1], c8(f_)[:, :, 0:1])
            step(v.memset(c8(suf)[:, :, CH - 1:CH], 1.0))
            for i in range(1, CH):
                j = CH - 1 - i
                tt(c8(pre)[:, :, i:i + 1], c8(pre)[:, :, i - 1:i], c8(f_)[:, :, i:i + 1], MUL)
                step(tt(c8(suf)[:, :, j:j + 1], c8(suf)[:, :, j + 1:j + 2], c8(f_)[:, :, j + 1:j + 2], MUL))
            tt(suf, suf, kf, MUL)
            tt(q_, q_, pre, MUL)
            for h in range(HG):
                last = v.memset(S_ST[:, 0, h, :], 0.0)
            last.then_inc(sem("ktil_ready"), 1)
            v.wait_ge(sem("ktil_ready"), 1)
            v.wait_ge(sem("s0_in"), 16)

            def turn(t):
                rows = TROWS[t]
                v.wait_ge(sem("turn_ps"), 2 * t + 1)
                cp(ktok[0:rows, t % 2, :], ps[7][0:rows, :]).then_inc(sem("turn_ev"), 1)
                v.wait_ge(sem("turn_ps"), 2 * t + 2)
                for c in range(4):
                    last = ts(vexp[0:rows, t % 2, c, :], ps[7][0:rows, :], const[0:rows, K_CM + c:K_CM + c + 1], None, MUL)
                last.then_inc(sem("turn_ev"), 1)

            def chain(G):
                for half in range(2):
                    u = 2 * G + half
                    v.wait_ge(sem("upd_ps"), u + 1)
                    for c in (2 * half, 2 * half + 1):
                        j = 4 * G + c
                        if G < 8:
                            if c == 3 and G >= 1:
                                v.wait_ge(sem("inter_ps"), G)
                            elif G >= 2:
                                v.wait_ge(sem("inter_ps"), G - 1)
                        elif c == 0:
                            v.wait_ge(sem("inter_ps"), G + 1)
                        for h in range(HG):
                            S = S_ST[:, j % 8, h, :] if G < 8 else S_END[:, j - 31, h, :]
                            So = (S_END[:, 0, h, :] if j == 31 else S_ST[:, (j + 1) % 8, h, :]) if G < 8 else S
                            U = ps[2 * (u % 2) + h // 2][:, 256 * (h % 2) + P * (c % 2):256 * (h % 2) + P * (c % 2) + P]
                            last = stt(So, S, pre[:, h, 8 * j + 7:8 * j + 8], U, MUL, ADD)
                        if c % 2 == 0:
                            step(last)
                    last.then_inc(sem("chain"), 1)
                    v.wait_ge(sem("chain"), u + 1)

            def inter(G):
                v.wait_ge(sem("inter_ps"), G + 1)
                tt(oB[:, :, 32 * G:32 * G + 32], oB[:, :, 32 * G:32 * G + 32],
                   ps[6][:, 0:128].rearrange("p (h n) -> p h n", h=HG), ADD).then_inc(sem("inter_ev"), 1)

            turn(0)
            beside = ADA_PIECES
            for G in range(NCHUNK // 4):
                if G < 8:
                    chain(G)
                if G % 4 == 1 and G // 4 + 1 < TT:
                    turn(G // 4 + 1)
                for _ in range(ADA_BESIDE[G]):
                    if beside > ADA_PIECES:
                        ada(beside - 1)
                    beside += 1
                inter(G)
                if G >= 8:
                    chain(G)
            ada(beside - 1)
            gains(1)
            v.wait_ge(sem("orms_ready"), 2)
            step(v.reciprocal(stat[:, 32:40], stat[:, 16:24]))
            step(v.reciprocal(stat[0:64, 40:44], stat[0:64, 24:28]))
            for t, rows in enumerate(TROWS):
                for h in range(HG):
                    c = 32 + 4 * t + h
                    last = ts(odiag[0:rows, t, h, :], ident[0:rows, :], stat[0:rows, c:c + 1], None, MUL)
            last.then_inc(sem("odiag_ready"), 1)
            v.wait_ge(sem("orstd_ready"), 1)
            step(stt(tlag, oB, cols[:, C_HGW:C_HGW + 1], banks[:, 0:4, 0:T], MUL, MUL))
            tt(mixT[:, 4:8, :], tlag, prj[:, 12:16, :], MUL).then_inc(sem("hgrn_done"), 1)
            v.wait_ge(sem("hgrn_done"), 1)

            v.memset(QX, 0.0)
            for n in range(9):
                t, rows = n % 3, TROWS[n % 3]
                v.wait_ge(sem("qkv_ps"), n + 1)
                src = ps[n % 6][0:rows, :]
                if n >= 6:
                    cp(vtok[0:rows, t, :], src).then_inc(sem("qkv_ev"), 1)
                    continue
                x = src.rearrange("p (h d) -> p h d", d=DH)
                a = rt1[0:rows, :].rearrange("p (h d) -> p h d", d=DH)
                b = rt2[0:rows, :].rearrange("p (h d) -> p h d", d=DH)
                cos = const[0:rows, K_COS + DH * t:K_COS + DH * t + DH]
                sin = const[0:rows, K_SIN + DH * t:K_SIN + DH * t + DH]
                tt(a, x, over(cos, HEADS, 1), MUL)
                tt(b[:, :, 0:32], x[:, :, 32:64], over(sin[:, 0:32], HEADS, 1), MUL)
                step(tt(b[:, :, 32:64], x[:, :, 0:32], over(sin[:, 32:64], HEADS, 1), MUL))
                dst = (qtok, ktk)[n // 3][0:rows, t, :]
                tt(dst, rt1[0:rows, :], rt2[0:rows, :], ADD).then_inc(sem("qkv_ev"), 1)
                v.wait_ge(sem("qkv_ev"), n + 1)
            for n in range(9, 15):
                w, t = (n - 9) // 3, n % 3
                rows = TROWS[t]
                v.wait_ge(sem("qkv_ps"), n + 1)
                cp(qkT[:, w, :, P * t:P * t + rows], ps[n % 6][:, :].rearrange("p (a n) -> p a n", a=4)[:, :, 0:rows])\
                    .then_inc(sem("qkv_ev"), 1)
            v.wait_ge(sem("qkv_ev"), 15)
            for p in range(PAIRS):
                for e in range(2):
                    last = cp(QX[64 * e:64 * e + 64, p, :, 16 * p + 8 * e:16 * p + 8 * e + 8],
                              bt(qkT[64 * e:64 * e + 64, 0, p, NP_TOK:T]))
            last.then_inc(sem("qx_ready"), 1)

            def prompt_front(h):
                s = sm[:, h % 2, :]
                v.wait_ge(sem("pscore_ps"), h + 1)
                x = sc[:, h % 2, :]
                stt(x, ps[h % 2][:, 0:384], SCALE, const[:, K_MP:K_MP + 384], MUL, ADD).then_inc(sem("pmask_done"), 1)
                v.wait_ge(sem("pmask_done"), h + 1)
                v.tensor_reduce(s[:, 2:3], x[:, 0:128], AX, MAX)
                step(v.tensor_reduce(s[:, 3:4], x[:, 128:384], AX, MAX))
                ts(s[:, 0:2], s[:, 2:4], -1.0, None, MUL).then_inc(sem("pmax_ready"), 1)

            def prompt_back(h):
                s, x = sm[:, h % 2, :], sc[:, h % 2, :]
                v.wait_ge(sem("pexp_ready"), 2 * h + 2)
                step(v.reciprocal(s[:, 6:8], s[:, 4:6]))
                ts(x[:, 0:128], x[:, 0:128], s[:, 6:7], None, MUL)
                ts(x[:, 128:384], x[:, 128:384], s[:, 7:8], None, MUL).then_inc(sem("p_ready"), 1)
                v.wait_ge(sem("pT_ps"), h + 1)
                if h >= 2:
                    v.wait_ge(sem("ppv_ps"), h - 1)
                cp(pT[:, h % 2, :], ps[2 + h % 2][:, 0:384]).then_inc(sem("pT_ready"), 1)
                if h % 2:
                    v.wait_ge(sem("ppv_ps"), h + 1)
                    cp(mixT[:, h // 2, 0:NP_TOK], ps[4 + h // 2 % 2][:, 0:NP_TOK]).then_inc(sem("ppv_ev"), 1)

            for h in range(HEADS + 1):
                if h < HEADS:
                    prompt_front(h)
                if h >= 1:
                    prompt_back(h - 1)

            for s in range(4):
                m, x = sm[:, s % 2, :], sc[:, s % 2, 0:320]
                v.wait_ge(sem("sscore_ps"), s + 1)
                ts(x[:, 0:256], ps[s % 2][:, 0:256], SCALE, None, MUL)
                stt(x[:, 256:320], ps[s % 2][:, 256:320], SCALE, const[:, K_MS + 64 * s:K_MS + 64 * s + 64], MUL, ADD)\
                    .then_inc(sem("smask_done"), 1)
                v.wait_ge(sem("smask_done"), s + 1)
                step(v.tensor_reduce(m[:, 2:3], x, AX, MAX))
                ts(m[:, 0:1], m[:, 2:3], -1.0, None, MUL).then_inc(sem("smax_ready"), 1)
                v.wait_ge(sem("sexp_ready"), s + 1)
                step(v.reciprocal(m[:, 6:7], m[:, 4:5]))
                ts(x, x, m[:, 6:7], None, MUL).then_inc(sem("s_ready"), 1)
                v.wait_ge(sem("sT_ps"), s + 1)
                cp(pT[:, s % 2, 0:256], ps[2 + s % 2][:, 0:256])
                cp(pT[0:64, s % 2, 256:384], ps[2 + s % 2][0:64, 256:384]).then_inc(sem("sT_ready"), 1)
                v.wait_ge(sem("spv_used"), 2 * s + 2)
                for e in range(2):
                    o = mixT[64 * e:64 * e + 64, 0:4, NP_TOK + 16 * s:NP_TOK + 16 * s + 16]\
                        .rearrange("p m (b t) -> p b m t", t=S_LEN)
                    i = ps[4 + s % 2][64 * e:64 * e + 64, 0:128].rearrange("p (b m n) -> p b m n", b=2, m=4)
                    last = cp(o, i[:, :, :, 8 * e:8 * e + 8])
                last.then_inc(sem("spv_ev"), 1)
            residual(0, "res0")
            norm(1)
            router(0)
            experts(0)
            norm(2)

            v.wait_ge(sem("hist_in"), 32)
            v.wait_ge(sem("hgrn_stored"), 16)
            v.memset(recP[:, :, 0:3], 0.0)
            cp(recS[:, :, :, 0:3], hist)
            L = [lsp[:, i, :] for i in range(6)]
            step(ts(L[2], cols[:, C_LAM:C_LAM + DT], -1.0, None, MUL))
            tt(L[0], L[2], cols[:, C_LAM:C_LAM + DT], MAX).then_inc(sem("lam_in"), 1)

            def conv(j):
                for m in range(DT):
                    w = cols[:, C_CONVW + 8 * j + m:C_CONVW + 8 * j + m + 1]
                    xp, xs = xc[:, m, 0:NP_TOK], bt(xc[:, m, NP_TOK:T])
                    rp, rs = recP[:, m, j:j + NP_TOK], recS[:, m, :, j:j + S_LEN]
                    if j == 0:
                        b = cols[:, C_CONVB + m:C_CONVB + m + 1]
                        ts(xp, rp, w, b, MUL, ADD)
                        last = ts(xs, rs, w, b, MUL, ADD)
                    else:
                        stt(xp, rp, w, xp, MUL, ADD)
                        last = stt(xs, rs, w, xs, MUL, ADD)
                last.then_inc(sem("conv_ready"), 1)
                v.wait_ge(sem("conv_ready"), j + 1)

            for n in range(16):
                v.wait_ge(sem("odd_ps"), n + 1)
                src, m = ps[n % 4], n % 8
                if n < 8:
                    cp(recP[:, m, 3:3 + NP_TOK], src[:, 0:NP_TOK])
                    cp(recS[:, m, :, 3:3 + S_LEN], bt(src[:, NP_TOK:T])).then_inc(sem("odd_ev"), 1)
                else:
                    cp(gT[:, m, :], src[:, 0:T]).then_inc(sem("odd_ev"), 1)
                    if n < 8 + CONV:
                        v.wait_ge(sem("odd_ev"), 8)
                        conv(n - 8)
            v.wait_ge(sem("odd_ev"), 16)
            c = float(np.sqrt(2.0 / np.pi))
            step(tt(t1, gT, gT, MUL))
            step(ts(t1, t1, 0.044715 * c, c, MUL, ADD))
            tt(t1, t1, gT, MUL).then_inc(sem("gelu_in"), 1)
            cp(cst[:, :, 0, :], recP[:, :, NP_TOK:NP_TOK + 3])
            cp(cst[:, :, 1:NSEQ, :], recS[:, :, :, S_LEN:S_LEN + 3])
            v.wait_ge(sem("lam_out"), 1)
            step(ts(L[3], L[1], 2.0, None, ADD))
            step(v.reciprocal(L[3], L[3]))
            step(tt(L[3], L[3], L[1], MUL))
            step(tt(L[4], L[3], L[3], MUL))
            step(ts(L[5], L[4], 1.0 / 17, 1.0 / 15, MUL, ADD))
            for k in range(13, 0, -2):
                step(tt(L[5], L[5], L[4], MUL))
                step(ts(L[5], L[5], 1.0 / k, None, ADD))
            step(tt(L[5], L[5], L[3], MUL))
            step(ts(L[2], L[2], 0.0, None, MAX))
            step(stt(L[5], L[5], 2.0, L[2], MUL, ADD))
            step(ts(L[5], L[5], -8.0, None, MUL))
            v.wait_ge(sem("gelu_out"), 1)
            stt(gT, t1, 1.0, gT, ADD, MUL)
            v.wait_ge(sem("lru_ev"), 16)
            tt(rT, rT, over(L[5], T), MUL).then_inc(sem("loga_ready"), 1)
            step(tt(iT, iT, xc, MUL))
            v.wait_ge(sem("a_ready"), 2)
            step(tt(hs, aT, aT, MUL))
            stt(t1, hs, 1.0, t1, ADD, MUL).then_inc(sem("om_ready"), 1)
            v.wait_ge(sem("root_ready"), 1)
            step(tt(t1, t1, iT, MUL))
            a0 = bt3(aT[:, :, NP_TOK:T])[:, :, :, 0]
            x0 = bt3(t1[:, :, NP_TOK:T])[:, :, :, 0]
            step(tt(lru0, lru0, a0, MUL))
            tt(x0, x0, lru0, ADD)
            v.memset(aT[:, :, 0:1], 0.0)
            step(v.memset(bt3(aT[:, :, NP_TOK:T])[:, :, :, 0:1], 0.0))
            step(v.tensor_tensor_scan(hs.rearrange("p m t -> p (m t)"), aT.rearrange("p m t -> p (m t)"),
                                      t1.rearrange("p m t -> p (m t)"), 0.0, MUL, ADD))
            cp(ends[:, :, 0:1], hs[:, :, NP_TOK - 1:NP_TOK])
            cp(ends[:, :, 1:NSEQ], bt3(hs[:, :, NP_TOK:T])[:, :, :, S_LEN - 1]).then_inc(sem("ends_ready"), 1)
            stt(xc, hs, 0.5, gT, MUL, MUL).then_inc(sem("odd_mix_ready"), 1)
            residual(2, "res1")
            norm(3)
            router(1)
            experts(1)
            norm(4)


_OUTS = {"yT": (P, DT, T), "k": (T, 512), "v": (T, 512), "hgrn": (P, NSEQ, HG, P),
         "convT": (P, DT, NSEQ, 3), "lruT": (P, DT, NSEQ)}


def shape_constants():
    f = np.float32
    K = np.zeros((P, N_CONST), f)
    K[:, K_ID:K_ID + P] = np.eye(P, dtype=f)
    half = DH // 2
    inv = np.power(f(10000.0), -np.arange(half, dtype=f) / f(half)).astype(f)
    pos = np.concatenate([np.arange(NP_TOK), np.tile(PAST_PAGES * PAGE + np.arange(S_LEN), NS_SEQ)]).astype(f)
    ang = np.zeros((TT * P, half), f)
    ang[:T] = pos[:, None] * inv[None, :]
    cos, sin = np.cos(ang).astype(f), np.sin(ang).astype(f)
    for t in range(TT):
        r = slice(P * t, P * t + P)
        K[:, K_COS + DH * t:K_COS + DH * t + DH] = np.concatenate([cos[r], cos[r]], 1)
        K[:, K_SIN + DH * t:K_SIN + DH * t + DH] = np.concatenate([-sin[r], sin[r]], 1)
    row, col = np.arange(P)[:, None], np.arange(2 * P)[None, :]
    K[:, K_MP:K_MP + 128] = np.where(col[:, :P] <= row, 0, FAR)
    K[:, K_MP + 128:K_MP + 384] = np.where(col <= row + P, 0, FAR)
    e, q = np.arange(P) // 64, np.arange(P) % 8
    for s in range(4):
        key = np.arange(64)[None, :]
        ok = (key // 8 == (2 * s + e)[:, None]) & (key % 8 <= q[:, None])
        K[:, K_MS + 64 * s:K_MS + 64 * s + 64] = np.where(ok, 0, FAR)
    for c in range(4):
        K[:, K_CM + c] = (np.arange(P) // CH % 4 == c)
    K[:, K_RANK:K_RANK + 4] = [4, 3, 2, 1]
    K[:, K_EPS] = EPS
    K[:, K_TRI:K_TRI + P] = row < np.arange(P)[None, :]
    K[:, K_IOTA:K_IOTA + P] = np.arange(P)
    K[:, K_SGN:K_SGN + NE] = np.where(np.arange(NE) % 2, -1, 1)
    K[:, K_OFF:K_OFF + NE] = np.where(np.arange(NE) % 2, SLOTS - 1, 0) + NOWHERE
    return K


def kernel(**a):
    import concourse.bacc as bacc
    from concourse.bass_utils import run_bass_kernel_spmd

    a = {k: np.asarray(x) for k, x in a.items()}

    def feat(x):
        return np.ascontiguousarray(x.reshape(x.shape[0], -1, P).transpose(2, 1, 0))

    def columns(x):
        return x.reshape(-1, P).T

    def pieces(w, n):
        k = w.shape[0] // P
        return w.reshape(k, P, -1, n).transpose(2, 1, 0, 3).reshape(-1, P, k * n)

    even = pieces(a["w_in_even"][0], 512)
    order = sorted([(i, w, e, n) for ws, w, n in ((W1, "moe_w1", 512), (W3, "moe_w3", 512), (W2, "moe_w2", 1024))
                    for e, i in enumerate(ws)])
    experts = [np.stack([pieces(a[w][l, e0 + e], n)[0] for e0 in range(0, NE, 4) for _, w, e, n in order])
               for l in range(2)]
    lru = np.stack([a["lru_wa"][0], a["lru_wx"][0]]).reshape(2, 4, 2, P, 256).transpose(3, 0, 1, 2, 4).reshape(1, P, PIECE)
    odd = pieces(a["w_in_odd"][0], 512)
    w = np.concatenate([pieces(a["ada_w"][0], 512), even[3:7], pieces(a["ada_w"][1], 512), even[0:3],
                        pieces(a["w_out_even"][0], 512), experts[0], odd[2:4], odd[0:2], lru,
                        pieces(a["w_out_odd"][0], 512), experts[1]])
    x = np.concatenate([a["x_prompt"].reshape(-1, D), a["x_sample"].reshape(-1, D)])
    c = np.concatenate([a["c_prompt"], a["c_sample"]])
    cols = np.concatenate([columns(a[n]) for n in ("ada_b", "norm_mix", "norm_ffn", "norm_final", "hg_lower_bounds",
                                                   "hg_norm_w", "conv_w", "conv_b", "lru_ba", "lru_bx", "lru_lambda")], 1)
    rw = np.concatenate([a["router_group_w"], a["router_expert_w"]], 2).reshape(2, DT, P, 20).transpose(2, 0, 1, 3)
    rb = np.concatenate([a["router_group_b"], a["router_expert_b"]], 1)[None]
    n_phys = a["cache_k"].shape[1]
    kT = a["cache_k"][0].reshape(n_phys, PAGE, PAIRS, P).transpose(0, 3, 2, 1).reshape(n_phys, P, 512)
    arrays = {
        "w": w, "xT": feat(x), "cT": feat(c), "cols": cols, "const": shape_constants(), "rw": rw, "rb": rb,
        "kT": kT, "v": a["cache_v"][0].reshape(n_phys, PAGE, 512),
        "s0": a["state_hgrn"][0].transpose(2, 0, 1, 3),
        "convT": a["state_conv"][0].reshape(NS_SEQ, 3, DT, P).transpose(3, 2, 0, 1),
        "lruT": feat(a["state_lru"][0]),
        "pages": a["page_table"].reshape(1, -1),
    }
    nc = bacc.Bacc("TRN2", target_bir_lowering=False, num_devices=1)
    arrays = {f"in_{k}": np.ascontiguousarray(x) for k, x in arrays.items()}
    I = {k[3:]: nc.dram_tensor(k, x.shape, mybir.dt.from_np(x.dtype), kind="ExternalInput").ap() for k, x in arrays.items()}
    O = {k: nc.dram_tensor(f"out_{k}", s, F32, kind="ExternalOutput").ap() for k, s in _OUTS.items()}
    build(nc, I, O)
    r = run_bass_kernel_spmd(nc, [arrays], core_ids=[0]).results[0]
    y = r["out_yT"].transpose(2, 1, 0).reshape(T, D)
    kv = [r[f"out_{n}"] for n in "kv"]
    hg = r["out_hgrn"].transpose(1, 2, 0, 3)[None]
    conv = r["out_convT"].transpose(2, 3, 1, 0).reshape(1, NSEQ, 3, D)
    lru = r["out_lruT"].transpose(2, 1, 0).reshape(1, NSEQ, D)
    C = np.ascontiguousarray
    return (C(y[:NP_TOK].reshape(1, NP_TOK, D)), C(y[NP_TOK:].reshape(NS_SEQ, S_LEN, D)),
            *(C(x[:NP_TOK].reshape(1, 1, NP_TOK, HEADS, DH)) for x in kv),
            *(C(x[NP_TOK:].reshape(1, NS_SEQ, S_LEN, HEADS, DH)) for x in kv),
            C(hg[:, :1]), C(hg[:, 1:]), C(conv[:, :1]), C(conv[:, 1:]), C(lru[:, :1]), C(lru[:, 1:]))
```
